# Optimizing a Trainium2 kernel written in Bass

```python
import jax, jax.numpy as jnp
from jax import lax
import numpy as np

D_MODEL = 1024
BATCH = 1
SEQ = 256
DEPTH = 2

CHUNK = 64
D_MIX = D_MODEL
POOL_WINDOWS = (2, 4, 8, 16)
N_POOL_GROUPS = len(POOL_WINDOWS)
D_POOL = D_MIX // 4
POOL_GC = D_POOL // N_POOL_GROUPS
D_SGU = D_MIX // 2
SGU_HEADS = 4
SGU_HD = D_SGU // SGU_HEADS
SGU_BLOCK = 128
D_CONV = D_MIX - D_POOL - D_SGU
CONV_W = 3
D_IN = D_POOL + 2 * D_SGU + 3 * D_CONV
SPLITS = (D_POOL, D_POOL + D_SGU, D_POOL + 2 * D_SGU, D_POOL + 2 * D_SGU + D_CONV, D_POOL + 2 * D_SGU + 2 * D_CONV)
D_FF = (7 * D_MODEL) // 2
N_EXPERTS = 8
TOP_K = 2
N_DENSE = (DEPTH + 1) // 2
N_MOE = DEPTH // 2
EPS = 1e-6


def rmsnorm(x, g):
    xf = x.astype(jnp.float32)
    y = xf * lax.rsqrt(jnp.mean(xf * xf, axis=-1, keepdims=True) + EPS)
    return (y * g.astype(jnp.float32)).astype(x.dtype)

def layernorm(x, g, b):
    xf = x.astype(jnp.float32)
    mu = jnp.mean(xf, axis=-1, keepdims=True)
    var = jnp.mean(jnp.square(xf - mu), axis=-1, keepdims=True)
    y = (xf - mu) * lax.rsqrt(var + EPS)
    return (y * g.astype(jnp.float32) + b.astype(jnp.float32)).astype(x.dtype)

def swiglu(h, w_gate, w_up, w_down):
    return (jax.nn.silu(h @ w_gate) * (h @ w_up)) @ w_down

def pool_mixer(a, pool_w, pool_scale):
    bsz, seq, _ = a.shape
    af = a.astype(jnp.float32).reshape(bsz, seq, N_POOL_GROUPS, POOL_GC)
    cs = jnp.cumsum(af, axis=1)
    pos = jnp.arange(seq)
    outs = []
    for g, w in enumerate(POOL_WINDOWS):
        c = cs[:, :, g]
        c_prev = jnp.pad(c, ((0, 0), (w, 0), (0, 0)))[:, :seq]
        count = jnp.minimum(pos + 1, w).astype(jnp.float32)[None, :, None]
        outs.append((c - c_prev) / count - af[:, :, g])
    d = jnp.stack(outs, axis=2).astype(a.dtype)
    y = jnp.einsum("bsgc,gcd->bsgd", d, pool_w)
    return y.reshape(bsz, seq, D_POOL) * pool_scale

def sgu_mixer(u, v, ln_g, ln_b, w_s, b_s):
    bsz, seq, _ = u.shape
    n_blk = seq // SGU_BLOCK
    vn = layernorm(v, ln_g, ln_b).reshape(bsz, n_blk, SGU_BLOCK, SGU_HEADS, SGU_HD)
    cid = jnp.arange(SGU_BLOCK) // CHUNK
    mask = (cid[:, None] >= cid[None, :]).astype(w_s.dtype)
    mixed = jnp.einsum("hij,bnjhc->bnihc", w_s * mask, vn) + b_s.T[None, None, :, :, None]
    return u * mixed.reshape(bsz, seq, D_SGU)

def short_conv_mixer(gb, gc, xc, conv_w):
    z = gc * xc
    zc = lax.conv_general_dilated(
        z, conv_w[:, None, :], window_strides=(1,), padding=[(CONV_W - 1, 0)],
        dimension_numbers=("NWC", "WIO", "NWC"), feature_group_count=D_CONV)
    return gb * zc

def token_mixer(h, w_in, pool_w, pool_scale, sgu_ln_g, sgu_ln_b, sgu_w, sgu_b, conv_w, group_g, w_out):
    p = h @ w_in
    a, u, v, gb, gc, xc = jnp.split(p, list(SPLITS), axis=-1)
    y_a = pool_mixer(a, pool_w, pool_scale)
    y_b = sgu_mixer(u, v, sgu_ln_g, sgu_ln_b, sgu_w, sgu_b)
    y_c = short_conv_mixer(gb, gc, xc, conv_w)
    y = jnp.concatenate([
        rmsnorm(y_a, group_g[:D_POOL]),
        rmsnorm(y_b, group_g[D_POOL:D_POOL + D_SGU]),
        rmsnorm(y_c, group_g[D_POOL + D_SGU:]),
    ], axis=-1)
    return y @ w_out

def moe_ffn(h, router_w, router_b, w_gate, w_up, w_down):
    bsz, seq, d = h.shape
    t = h.reshape(bsz * seq, d)
    logits = t.astype(jnp.float32) @ router_w.astype(jnp.float32) + router_b.astype(jnp.float32)
    top_v, top_i = lax.top_k(logits, TOP_K)
    gates = jax.nn.softmax(top_v, axis=-1)
    combine = jnp.sum(jax.nn.one_hot(top_i, N_EXPERTS, dtype=jnp.float32) * gates[..., None], axis=1)
    out = jnp.zeros((bsz * seq, d), jnp.float32)
    for e in range(N_EXPERTS):
        y_e = swiglu(t, w_gate[e], w_up[e], w_down[e])
        out = out + combine[:, e:e + 1] * y_e.astype(jnp.float32)
    return out.astype(h.dtype).reshape(bsz, seq, d)

def first_inputs(seed: int = 0) -> dict:
    key = jax.random.key(seed)
    ks = jax.random.split(key, 24)

    def nrm(k, shape, scale):
        return jax.random.normal(k, shape, jnp.float32) * scale

    return {
        "x": nrm(ks[0], (BATCH, SEQ, D_MODEL), 1.0),
        "norm1_g": 1.0 + nrm(ks[1], (DEPTH, D_MODEL), 0.05),
        "w_in": nrm(ks[2], (DEPTH, D_MODEL, D_IN), D_MODEL ** -0.5),
        "pool_w": nrm(ks[3], (DEPTH, N_POOL_GROUPS, POOL_GC, POOL_GC), POOL_GC ** -0.5),
        "pool_scale": 1.0 + nrm(ks[4], (DEPTH, D_POOL), 0.1),
        "sgu_ln_g": 1.0 + nrm(ks[5], (DEPTH, D_SGU), 0.05),
        "sgu_ln_b": nrm(ks[6], (DEPTH, D_SGU), 0.02),
        "sgu_w": nrm(ks[7], (DEPTH, SGU_HEADS, SGU_BLOCK, SGU_BLOCK), SGU_BLOCK ** -0.5),
        "sgu_b": 1.0 + nrm(ks[8], (DEPTH, SGU_HEADS, SGU_BLOCK), 0.05),
        "conv_w": nrm(ks[9], (DEPTH, CONV_W, D_CONV), CONV_W ** -0.5),
        "group_g": 1.0 + nrm(ks[10], (DEPTH, D_MIX), 0.05),
        "w_out": nrm(ks[11], (DEPTH, D_MIX, D_MODEL), D_MIX ** -0.5),
        "norm2_g": 1.0 + nrm(ks[12], (DEPTH, D_MODEL), 0.05),
        "ffn_w_gate": nrm(ks[13], (N_DENSE, D_MODEL, D_FF), D_MODEL ** -0.5),
        "ffn_w_up": nrm(ks[14], (N_DENSE, D_MODEL, D_FF), D_MODEL ** -0.5),
        "ffn_w_down": nrm(ks[15], (N_DENSE, D_FF, D_MODEL), D_FF ** -0.5),
        "router_w": nrm(ks[16], (N_MOE, D_MODEL, N_EXPERTS), D_MODEL ** -0.5),
        "router_b": nrm(ks[17], (N_MOE, N_EXPERTS), 0.01),
        "moe_w_gate": nrm(ks[18], (N_MOE, N_EXPERTS, D_MODEL, D_FF), D_MODEL ** -0.5),
        "moe_w_up": nrm(ks[19], (N_MOE, N_EXPERTS, D_MODEL, D_FF), D_MODEL ** -0.5),
        "moe_w_down": nrm(ks[20], (N_MOE, N_EXPERTS, D_FF, D_MODEL), D_FF ** -0.5),
        "final_g": 1.0 + nrm(ks[21], (D_MODEL,), 0.05),
    }

def first_block(x, norm1_g, w_in, pool_w, pool_scale, sgu_ln_g, sgu_ln_b, sgu_w, sgu_b, conv_w,
              group_g, w_out, norm2_g, ffn_w_gate, ffn_w_up, ffn_w_down, router_w, router_b,
              moe_w_gate, moe_w_up, moe_w_down, final_g):
    for l in range(DEPTH):
        h = rmsnorm(x, norm1_g[l])
        x = x + token_mixer(h, w_in[l], pool_w[l], pool_scale[l], sgu_ln_g[l], sgu_ln_b[l],
                            sgu_w[l], sgu_b[l], conv_w[l], group_g[l], w_out[l])
        h = rmsnorm(x, norm2_g[l])
        j = l // 2
        if l % 2 == 0:
            x = x + swiglu(h, ffn_w_gate[j], ffn_w_up[j], ffn_w_down[j])
        else:
            x = x + moe_ffn(h, router_w[j], router_b[j], moe_w_gate[j], moe_w_up[j], moe_w_down[j])
    return rmsnorm(x, final_g)


Q_BLOCK = 128
D_MIX_2 = D_MODEL
N_HEADS = 8
QK_NOPE = 64
QK_ROPE = 32
QK_DIM = QK_NOPE + QK_ROPE
V_DIM = 64
Q_LORA = 384
KV_LORA = 256
ATTN_W = N_HEADS * V_DIM
CONV_W_2 = D_MIX_2 - ATTN_W
CONV_K = 31
D_FF_2 = 2816
ROPE_THETA = 10000.0
IN_COLS = Q_LORA + KV_LORA + QK_ROPE + 2 * CONV_W_2


def rms_norm(x, g):
    xf = x.astype(jnp.float32)
    y = xf * lax.rsqrt(jnp.mean(xf * xf, axis=-1, keepdims=True) + EPS)
    return (y * g.astype(jnp.float32)).astype(x.dtype)

def layer_norm(x, g, b):
    xf = x.astype(jnp.float32)
    mu = jnp.mean(xf, axis=-1, keepdims=True)
    xc = xf - mu
    y = xc * lax.rsqrt(jnp.mean(xc * xc, axis=-1, keepdims=True) + EPS)
    return (y * g.astype(jnp.float32) + b.astype(jnp.float32)).astype(x.dtype)

def swiglu_2(x, w_gate, w_up, w_down):
    return (jax.nn.silu(x @ w_gate) * (x @ w_up)) @ w_down

def rope_tables(seq_len):
    pos = jnp.arange(seq_len, dtype=jnp.float32)
    inv_freq = 1.0 / (ROPE_THETA ** (jnp.arange(0, QK_ROPE, 2, dtype=jnp.float32) / QK_ROPE))
    ang = pos[:, None] * inv_freq[None, :]
    return jnp.cos(ang), jnp.sin(ang)

def apply_rope(x, cos, sin):
    xf = x.astype(jnp.float32)
    half = QK_ROPE // 2
    x1, x2 = xf[..., :half], xf[..., half:]
    c, s = cos[None, :, None, :], sin[None, :, None, :]
    out = jnp.concatenate([x1 * c - x2 * s, x1 * s + x2 * c], axis=-1)
    return out.astype(x.dtype)

def chunk_causal_attention(q, k, v):
    b, h, s, _ = q.shape
    scale = QK_DIM ** -0.5
    outs = []
    for i in range(s // Q_BLOCK):
        q0 = i * Q_BLOCK
        k_end = q0 + Q_BLOCK
        qs = q[:, :, q0:k_end]
        ks = k[:, :, :k_end]
        vs = v[:, :, :k_end]
        scores = jnp.einsum('bhqd,bhkd->bhqk', qs, ks).astype(jnp.float32) * scale
        q_chunk = (q0 + jnp.arange(Q_BLOCK)) // CHUNK
        k_chunk = jnp.arange(k_end) // CHUNK
        allowed = k_chunk[None, :] <= q_chunk[:, None]
        scores = jnp.where(allowed[None, None], scores, -1e30)
        probs = jax.nn.softmax(scores, axis=-1).astype(vs.dtype)
        outs.append(jnp.einsum('bhqk,bhkd->bqhd', probs, vs))
    out = jnp.concatenate(outs, axis=1)
    return out.reshape(b, s, h * V_DIM)

def mla_group(c_q_raw, c_kv_raw, k_pe_raw, q_lat_g, w_uq, kv_lat_g, w_ukv, q_g, k_g, cos, sin):
    b, s, _ = c_q_raw.shape
    q = (rms_norm(c_q_raw, q_lat_g) @ w_uq).reshape(b, s, N_HEADS, QK_DIM)
    kv = (rms_norm(c_kv_raw, kv_lat_g) @ w_ukv).reshape(b, s, N_HEADS, QK_NOPE + V_DIM)
    k_nope, v = kv[..., :QK_NOPE], kv[..., QK_NOPE:]
    k_pe = jnp.broadcast_to(k_pe_raw[:, :, None, :], (b, s, N_HEADS, QK_ROPE))
    k = jnp.concatenate([k_nope, k_pe], axis=-1)
    q = rms_norm(q, q_g)
    k = rms_norm(k, k_g)
    q = jnp.concatenate([q[..., :QK_NOPE], apply_rope(q[..., QK_NOPE:], cos, sin)], axis=-1)
    k = jnp.concatenate([k[..., :QK_NOPE], apply_rope(k[..., QK_NOPE:], cos, sin)], axis=-1)
    q = jnp.transpose(q, (0, 2, 1, 3))
    k = jnp.transpose(k, (0, 2, 1, 3))
    v = jnp.transpose(v, (0, 2, 1, 3))
    return chunk_causal_attention(q, k, v)

def conv_group(u_raw, conv_w, conv_b, ln_g, ln_b):
    a, g = u_raw[..., :CONV_W_2], u_raw[..., CONV_W_2:]
    u = a * jax.nn.sigmoid(g)
    y = lax.conv_general_dilated(
        u, conv_w[:, None, :].astype(u.dtype),
        window_strides=(1,), padding=[(CONV_K - 1, 0)],
        dimension_numbers=('NWC', 'WIO', 'NWC'),
        feature_group_count=CONV_W_2)
    y = y + conv_b
    return jax.nn.silu(layer_norm(y, ln_g, ln_b))

def second_inputs(seed: int = 0) -> dict:
    key = jax.random.key(seed)
    ks = jax.random.split(key, 24)
    L, D, F = DEPTH, D_MODEL, D_FF_2

    def w(k, shape, fan_in):
        return jax.random.normal(k, shape, jnp.float32) * (fan_in ** -0.5)

    def gain(k, shape):
        return 1.0 + 0.02 * jax.random.normal(k, shape, jnp.float32)

    def bias(k, shape):
        return 0.02 * jax.random.normal(k, shape, jnp.float32)

    return {
        "x": jax.random.normal(ks[0], (BATCH, SEQ, D), jnp.float32),
        "ffn1_norm": gain(ks[1], (L, D)),
        "ffn1_w_gate": w(ks[2], (L, D, F), D),
        "ffn1_w_up": w(ks[3], (L, D, F), D),
        "ffn1_w_down": w(ks[4], (L, F, D), F),
        "mix_norm": gain(ks[5], (L, D)),
        "w_in": w(ks[6], (L, D, IN_COLS), D),
        "q_latent_norm": gain(ks[7], (L, Q_LORA)),
        "w_uq": w(ks[8], (L, Q_LORA, N_HEADS * QK_DIM), Q_LORA),
        "kv_latent_norm": gain(ks[9], (L, KV_LORA)),
        "w_ukv": w(ks[10], (L, KV_LORA, N_HEADS * (QK_NOPE + V_DIM)), KV_LORA),
        "q_norm": gain(ks[11], (L, QK_DIM)),
        "k_norm": gain(ks[12], (L, QK_DIM)),
        "conv_w": w(ks[13], (L, CONV_K, CONV_W_2), CONV_K),
        "conv_b": bias(ks[14], (L, CONV_W_2)),
        "conv_ln_g": gain(ks[15], (L, CONV_W_2)),
        "conv_ln_b": bias(ks[16], (L, CONV_W_2)),
        "w_out": w(ks[17], (L, D_MIX_2, D), D_MIX_2),
        "ffn2_norm": gain(ks[18], (L, D)),
        "ffn2_w_gate": w(ks[19], (L, D, F), D),
        "ffn2_w_up": w(ks[20], (L, D, F), D),
        "ffn2_w_down": w(ks[21], (L, F, D), F),
        "post_norm": gain(ks[22], (L, D)),
    }

def second_block(x, ffn1_norm, ffn1_w_gate, ffn1_w_up, ffn1_w_down, mix_norm, w_in,
              q_latent_norm, w_uq, kv_latent_norm, w_ukv, q_norm, k_norm,
              conv_w, conv_b, conv_ln_g, conv_ln_b, w_out,
              ffn2_norm, ffn2_w_gate, ffn2_w_up, ffn2_w_down, post_norm):
    cos, sin = rope_tables(x.shape[1])
    o_kv = Q_LORA
    o_pe = Q_LORA + KV_LORA
    o_cv = Q_LORA + KV_LORA + QK_ROPE
    for l in range(DEPTH):
        x = x + 0.5 * swiglu_2(rms_norm(x, ffn1_norm[l]), ffn1_w_gate[l], ffn1_w_up[l], ffn1_w_down[l])
        h = rms_norm(x, mix_norm[l])
        p = h @ w_in[l]
        attn = mla_group(p[..., :o_kv], p[..., o_kv:o_pe], p[..., o_pe:o_cv],
                         q_latent_norm[l], w_uq[l], kv_latent_norm[l], w_ukv[l],
                         q_norm[l], k_norm[l], cos, sin)
        conv = conv_group(p[..., o_cv:], conv_w[l], conv_b[l], conv_ln_g[l], conv_ln_b[l])
        x = x + jnp.concatenate([attn, conv], axis=-1) @ w_out[l]
        x = x + 0.5 * swiglu_2(rms_norm(x, ffn2_norm[l]), ffn2_w_gate[l], ffn2_w_up[l], ffn2_w_down[l])
        x = rms_norm(x, post_norm[l])
    return x


def setup_inputs(seed=0):
    out = dict(first_inputs(seed))
    for name, value in second_inputs(seed + 1).items():
        if name != "x":
            out[name + "_2"] = value
    return out


def reference(
    x, norm1_g, w_in, pool_w, pool_scale, sgu_ln_g, sgu_ln_b, sgu_w, sgu_b, conv_w, group_g,
    w_out, norm2_g, ffn_w_gate, ffn_w_up, ffn_w_down, router_w, router_b, moe_w_gate, moe_w_up,
    moe_w_down, final_g, ffn1_norm_2, ffn1_w_gate_2, ffn1_w_up_2, ffn1_w_down_2, mix_norm_2,
    w_in_2, q_latent_norm_2, w_uq_2, kv_latent_norm_2, w_ukv_2, q_norm_2, k_norm_2, conv_w_2,
    conv_b_2, conv_ln_g_2, conv_ln_b_2, w_out_2, ffn2_norm_2, ffn2_w_gate_2, ffn2_w_up_2,
    ffn2_w_down_2, post_norm_2,
):
    x = first_block(
        x, norm1_g, w_in, pool_w, pool_scale, sgu_ln_g, sgu_ln_b, sgu_w, sgu_b, conv_w, group_g,
        w_out, norm2_g, ffn_w_gate, ffn_w_up, ffn_w_down, router_w, router_b, moe_w_gate,
        moe_w_up, moe_w_down, final_g,
    )
    return second_block(
        x, ffn1_norm_2, ffn1_w_gate_2, ffn1_w_up_2, ffn1_w_down_2, mix_norm_2, w_in_2,
        q_latent_norm_2, w_uq_2, kv_latent_norm_2, w_ukv_2, q_norm_2, k_norm_2, conv_w_2,
        conv_b_2, conv_ln_g_2, conv_ln_b_2, w_out_2, ffn2_norm_2, ffn2_w_gate_2, ffn2_w_up_2,
        ffn2_w_down_2, post_norm_2,
    )


_drawn_inputs = setup_inputs


def setup_inputs(seed=0):
    import zlib

    import numpy as np

    out = dict(_drawn_inputs(seed))
    spreads = {}
    factors = {'sgu_ln_b': 2.846,
     'router_b': 3.614,
     'ffn1_norm_2': 4.349,
     'mix_norm_2': 4.208,
     'q_latent_norm_2': 8.0,
     'kv_latent_norm_2': 8.0,
     'q_norm_2': 8.0,
     'k_norm_2': 8.0,
     'conv_ln_g_2': 4.111,
     'conv_ln_b_2': 4.411,
     'ffn2_norm_2': 5.109}
    for name, (base, spread) in spreads.items():
        noise = np.random.default_rng([zlib.crc32(name.encode()), seed]).standard_normal(out[name].shape)
        drawn = base * np.exp(spread * noise) if base else spread * noise
        out[name] = __import__('jax').numpy.asarray(drawn.astype(out[name].dtype))
    for name, factor in factors.items():
        out[name] = (out[name] * factor).astype(out[name].dtype)
    return out
```

```python
from contextlib import ExitStack

import numpy as np
import concourse.bass as bass
from concourse import mybir

F32 = mybir.dt.float32
F32R = mybir.dt.float32r
I32 = mybir.dt.int32
ACT = mybir.ActivationFunctionType
ALU = mybir.AluOpType
AX = mybir.AxisListType.X

P = 128
T = 256
TT = T // P
D = 1024
KD = D // P
F1 = 3584
F2 = 2816
FW = 256
NE = 8
PIECE = KD * FW
RING = 3
EPS = 1e-6
DP, DS, DC = 256, 512, 256
WINDOWS = (2, 4, 8, 16)
PAD = 16
SH = 4
CW = 3
NH, QK, NOPE, ROPE, VD = 8, 96, 64, 32, 64
QL, KVL = 384, 256
CK = 31
CPAD = CK - 1
TOKW = QL + KVL + ROPE
NEG = -1e30
SCALE = float(QK) ** -0.5
THETA = 10000.0

STEPS1 = F1 // FW
STEPS2 = F2 // FW
EXPERT_PIECES = 3 * STEPS1


def rope_tables():
    pos = np.arange(T, dtype=np.float32)
    inv = (1.0 / (THETA ** (np.arange(0, ROPE, 2, dtype=np.float32) / ROPE))).astype(np.float32)
    ang = (pos[:, None] * inv[None, :]).astype(np.float32)
    return np.concatenate([np.cos(ang), np.sin(ang)], axis=1).astype(np.float32)


def plan():
    kinds, stages = [], []
    steps = rows = cols = norms = 0

    def ffn(name, layer, n, experts=1):
        nonlocal steps, rows, norms
        stages.append(dict(kind=name, layer=layer, n=n, B=len(kinds), S=steps, R=rows, C=cols, M=norms))
        norms += 1
        for _ in range(experts):
            kinds.extend(["gate", "up"] + ["gate", "up", "rows"] * (n - 1) + ["rows"])
        steps += n * experts
        rows += n * experts

    def mixer(name, layer, ncols):
        nonlocal rows, norms, cols
        stages.append(dict(kind=name, layer=layer, B=len(kinds), S=steps, R=rows, C=cols, M=norms))
        norms += 1
        kinds.extend(["cols"] * ncols + ["rows"] * 4)
        rows += 4
        cols += ncols

    for l in range(2):
        mixer("mix1", l, 8)
        if l == 0:
            ffn("ffn1", 0, STEPS1)
        else:
            ffn("moe", 0, STEPS1, NE)
    stages.append(dict(kind="post", layer=0))
    for l in range(2):
        ffn("ffn2a", l, STEPS2)
        mixer("mix2", l, 10)
        ffn("ffn2b", l, STEPS2)
        stages.append(dict(kind="post", layer=1 + l))
    q = 0
    for s in stages:
        s["Q"] = q
        q += 1
    return kinds, stages


def build(nc, A, rope, out):
    kinds, stages = plan()

    with ExitStack() as ctx:
        def sb(name, shape, dt=F32):
            return ctx.enter_context(nc.sbuf_tensor(name, shape, dt))

        def sem(name):
            return ctx.enter_context(nc.semaphore(name))

        raw = sb("raw", [P, RING, PIECE])
        hi = sb("hi", [P, RING, PIECE], F32R)
        lo = sb("lo", [P, RING, PIECE], F32R)
        x = sb("x", [P, TT, D])
        xn = sb("xn", [P, TT, D])
        xh = sb("xh", [P, KD, T], F32R)
        xl = sb("xl", [P, KD, T], F32R)
        sg = sb("sg", [P, 2, T])
        hf = sb("hf", [P, 2, T])
        hh = sb("hh", [P, 2, T], F32R)
        hl = sb("hl", [P, 2, T], F32R)
        ident = sb("ident", [P, P])
        ones = sb("ones", [P, P])
        before = sb("before", [P, P])
        slots = sb("slots", [P, P])
        zeros = sb("zeros", [P, 512], F32R)
        earlier = sb("earlier", [P, NE, NE])
        invc = sb("invc", [P, 2, T])
        chan = sb("chan", [P, 4, P])
        ropet = sb("ropet", [P, TT, ROPE])
        vecs = sb("vecs", [P, 3, D])
        lng = sb("lng", [P, DS])
        lnb = sb("lnb", [P, DS])
        psc = sb("psc", [P, DP])
        poolw = sb("poolw", [P, 2, 2, P])
        wsT = sb("wsT", [P, 2, SH, P])
        qkg = sb("qkg", [P, 2, 2, QK])
        routw = sb("routw", [P, KD, NE])
        rwh = sb("rwh", [P, KD, NE], F32R)
        rwl = sb("rwl", [P, KD, NE], F32R)
        routb = sb("routb", [P, NE])
        ssq = sb("ssq", [P, 8])
        var = sb("var", [P, 8])
        std = sb("std", [P, 8])
        rstd = sb("rstd", [P, 8])
        bns = sb("bns", [P, TT, 2, 6])
        bna = sb("bna", [P, TT, 2])
        hsq = sb("hsq", [P, TT * 2 * NH])
        hvar = sb("hvar", [P, TT * 2 * NH])
        hstd = sb("hstd", [P, TT * 2 * NH])
        hrstd = sb("hrstd", [P, TT * 2 * NH])
        nmax = sb("nmax", [P, TT * NH])
        psum_p = sb("psum_p", [P, TT * NH])
        rsum = sb("rsum", [P, TT, NH])
        negm = sb("negm", [P, TT * NH])
        logit = sb("logit", [P, TT, NE])
        big = sb("big", [P, TT, NE * NE])
        big2 = sb("big2", [P, TT, NE * NE])
        place = sb("place", [P, TT, NE])
        sel = sb("sel", [P, TT, NE])
        top = sb("top", [P, TT])
        ex = sb("ex", [P, TT, NE])
        den = sb("den", [P, TT])
        rden = sb("rden", [P, TT])
        gates = sb("gates", [P, TT, NE])
        rank = sb("rank", [P, TT, 2, NE + 1])
        most = sb("most", [P, 1])
        spill = sb("spill", [1, 1], I32)
        touch = sb("touch", [P, 32])
        ptouch = sb("ptouch", [P, 1])

        ARENA = 53 * 1024
        arena = sb("arena", [P, ARENA // 4])
        base = nc.sbuf_base - ARENA

        class Scratch:
            def __init__(self):
                self.at = 0

            def __call__(self, name, shape, dt=F32):
                t = nc.alloc_sbuf_tensor_at(name, shape, dt, offset=base + self.at)
                self.at += 4 * int(np.prod(shape[1:]))
                self.at += -self.at % 32
                assert self.at <= ARENA, (name, self.at)
                return t

        s0 = Scratch()
        stage_rows = s0("stage_rows", [P, 4, P])
        stage_ws = s0("stage_ws", [P, 2, SH, P])
        s1 = Scratch()
        apad = s1("apad", [P, 2, PAD + T])
        w2 = s1("w2", [P, 2, PAD + T])
        w4 = s1("w4", [P, 2, PAD + T])
        w8 = s1("w8", [P, 2, PAD + T])
        w16 = s1("w16", [P, 2, PAD + T])
        dT = s1("dT", [P, 2, T])
        gcT = s1("gcT", [P, 2, T])
        zpad = s1("zpad", [P, 2, CW - 1 + T])
        zc = s1("zc", [P, 2, T])
        gb = s1("gb", [P, TT, DC])
        u1 = s1("u1", [P, TT, DS])
        vn = s1("vn", [P, TT, DS])
        y1 = s1("y1", [P, TT, D])
        s2 = Scratch()
        h2h = s2("h2h", [P, TT, D], F32R)
        h2l = s2("h2l", [P, TT, D], F32R)
        yh = s2("yh", [P, D], F32R)
        yl = s2("yl", [P, D], F32R)
        pick = s2("pick", [P, TT, P], F32R)
        pickT = s2("pickT", [P, T], F32R)
        s3 = Scratch()
        ptok = s3("ptok", [P, TT, TOKW])
        qk = s3("qk", [P, TT, 2 * NH, QK])
        v2 = s3("v2", [P, TT, NH, VD])
        upad = s3("upad", [P, 4, CPAD + T])
        acc = s3("acc", [P, 4, T])
        prob = s3("prob", [P, 2, 3 * P])
        probT = s3("probT", [P, 2, 3 * P])
        at_qkT = s3.at
        qkT = s3("qkT", [P, 2 * NH, T])
        s3.at = at_qkT
        sq2 = s3("sq2", [P, TT, 2 * NH, QK])
        s3.at = at_qkT
        rt = s3("rt", [P, 4, TT, 2 * NH, ROPE // 2])

        bank = [ctx.enter_context(nc.psum_tensor(f"bank{i}", [P, 512], F32)) for i in range(8)]
        DOWN = (2, 3, 4, 5)
        GATE, UP = 0, 1

        class Ring:

            def __init__(self, tag):
                self.raw_full = [sem(f"{tag}raw_full{s}") for s in range(RING)]
                self.hi_done = sem(f"{tag}hi_done")
                self.lo_done = sem(f"{tag}lo_done")
                self.done = {k: sem(f"{tag}{k}_done") for k in ("gate", "up", "rows", "cols")}
                self.sg_done = sem(f"{tag}sg_done")
                self.hf_done = sem(f"{tag}hf_done")
                self.hh_done = sem(f"{tag}hh_done")
                self.hl_done = sem(f"{tag}hl_done")
                self.pick_done = sem(f"{tag}pick_done")
                self.gathered = sem(f"{tag}gathered")
                self.gh_done = sem(f"{tag}gh_done")
                self.gl_done = sem(f"{tag}gl_done")
                self.pick_turned = sem(f"{tag}pick_turned")
                self.pickT_done = sem(f"{tag}pickT_done")
                self.yh_done = sem(f"{tag}yh_done")
                self.yl_done = sem(f"{tag}yl_done")
                self.spread = sem(f"{tag}spread")
                self.added = sem(f"{tag}added")

        main = Ring("")
        again = Ring("spill_")
        x_loaded = sem("x_loaded")
        x_done = sem("x_done")
        ssq_done = sem("ssq_done")
        var_done = sem("var_done")
        std_done = sem("std_done")
        xn_done = sem("xn_done")
        turned = sem("turned")
        xh_done = sem("xh_done")
        xl_done = sem("xl_done")
        chain = sem("chain")
        achain = sem("achain")
        pchain = sem("pchain")
        stored = sem("stored")
        E = {}

        def ev(name):
            if name not in E:
                E[name] = sem(name)
            return E[name]

        def done_of(n):
            return main.done[kinds[n]], kinds[:n + 1].count(kinds[n])

        staged, where, used = [], {}, [0, 0, 0, 0]

        def put(tile, name, ap, n):
            staged.append((tile, used[tile], n, ap.rearrange("(r c) -> r c", c=P)))
            where[name] = (tile, used[tile])
            used[tile] += n

        for l in range(2):
            put(0, ("norm1", l), A["norm1_g"][l], KD)
            put(0, ("norm2", l), A["norm2_g"][l], KD)
            put(0, ("group", l), A["group_g"][l], KD)
            put(0, ("ffn1", l), A["ffn1_norm_2"][l], KD)
            put(0, ("mix", l), A["mix_norm_2"][l], KD)
            put(0, ("ffn2", l), A["ffn2_norm_2"][l], KD)
            put(1, ("cw", l), A["conv_w"][l].rearrange("a c -> (a c)"), CW * 2)
            put(1, ("cb", l), A["conv_b_2"][l], 4)
            put(1, ("clg", l), A["conv_ln_g_2"][l], 4)
            put(1, ("clb", l), A["conv_ln_b_2"][l], 4)
            put(1, ("ql", l), A["q_latent_norm_2"][l], QL // P)
            put(1, ("kvl", l), A["kv_latent_norm_2"][l], KVL // P)
            put(1, ("sb", l), A["sgu_b"][l].rearrange("h i -> (h i)"), SH)
            put(2 + l, ("cw2", l), A["conv_w_2"][l].rearrange("a c -> (a c)"), CK * 4)

        def col(name, i):
            tile, at = where[name]
            return chan[:, tile, at + i:at + i + 1]

        norm_gain = {"mix1": "norm1", "ffn1": "norm2", "moe": "norm2", "ffn2a": "ffn1", "mix2": "mix", "ffn2b": "ffn2"}

        def gain_of(st, k):
            return col((norm_gain[st["kind"]], 1 if st["kind"] == "moe" else st["layer"]), k)

        def cols_view(w):
            return w.rearrange("(k p) f -> p k f", p=P)

        def rows_view(w):
            return w.rearrange("(s p) d -> p s d", p=P)

        def weights_of(st):
            l = st["layer"]
            if st["kind"] == "ffn1":
                return A["ffn_w_gate"][0], A["ffn_w_up"][0], A["ffn_w_down"][0]
            w = "ffn1" if st["kind"] == "ffn2a" else "ffn2"
            return A[f"{w}_w_gate_2"][l], A[f"{w}_w_up_2"][l], A[f"{w}_w_down_2"][l]

        MIX1_COLS = (768, 1024, 0, 1536, 1792, 1280, 256, 512)
        MIX1_BANKS = (0, 1, 6, 7, 2, 3, 4, 5)
        MIX2_COLS = ((0, 256), (256, 256), (512, 160), (672, 256), (928, 256), (1184, 256), (1440, 256))
        MIX2_BANKS = (0, 1, 6, 7, 2, 3, 4)
        Q_BANKS = ((6, 7), (2, 3))
        KV_BANKS = ((4, 5), (0, 1))
        TURN4 = (6, 7, 2, 3)
        Y_BANKS = (0, 1, 6, 7)
        CAT_BANKS = (0, 1, 4, 5)
        END = sum(1 for _ in kinds)
        moe = next(s for s in stages if s["kind"] == "moe")
        MOE_END = moe["B"] + NE * EXPERT_PIECES

        def bank_end(c, n):
            return min(n, c // 2 * 2 + 2)

        def gate_ps(w):
            return bank[GATE][:, 0:2 * w].rearrange("p (s t) -> p s t", s=2)

        def up_ps(w):
            return bank[UP][:, 0:2 * w].rearrange("p (s t) -> p s t", s=2)

        SPILL = dict(kind="moe", layer=0, n=STEPS1, B=RING, S=0, R=1)

        def sp_load(sp, S, c, i, src, shape):
            n = shape[0] * shape[1]
            if c >= RING:
                sp.wait_ge(S.lo_done, c - RING + 1 + 3 * i)
            dst = raw[:, c % RING, 0:n].rearrange("p (a b) -> p a b", a=shape[0])
            sp.dma_start(dst, src).then_inc(S.raw_full[c % RING], 16)

        def sp_ffn(sp, S, B, n, wg, wu, wd, i0=0):
            sp_load(sp, S, B, i0, wg[:, :, 0:FW], (KD, FW))
            sp_load(sp, S, B + 1, i0, wu[:, :, 0:FW], (KD, FW))
            with sp.Fori(1, n) as j:
                sp_load(sp, S, B - 1, i0 + j, wg[:, :, bass.ds(j * FW, FW)], (KD, FW))
                sp_load(sp, S, B, i0 + j, wu[:, :, bass.ds(j * FW, FW)], (KD, FW))
                sp_load(sp, S, B + 1, i0 + j, wd[:, bass.ds((j - 1) * 2, 2), :], (2, D))
            sp_load(sp, S, B + 3 * n - 1, i0, wd[:, 2 * (n - 1):2 * n, :], (2, D))

        def sp_experts(sp, S, st):
            wg = A["moe_w_gate"][0].rearrange("e (k p) f -> e p k f", p=P)
            wu = A["moe_w_up"][0].rearrange("e (k p) f -> e p k f", p=P)
            wd = A["moe_w_down"][0].rearrange("e (s p) d -> e p s d", p=P)
            with sp.Fori(0, NE) as e:
                sp_ffn(sp, S, st["B"], STEPS1, wg[e], wu[e], wd[e], STEPS1 * e)

        block = ctx.enter_context(nc.Block())

        @block.sync
        def _(sp):
            for st in stages:
                k, l = st["kind"], st["layer"]
                if k == "mix1":
                    w = cols_view(A["w_in"][l])
                    for m, c0 in enumerate(MIX1_COLS):
                        sp_load(sp, main, st["B"] + m, 0, w[:, :, c0:c0 + FW], (KD, FW))
                    w = rows_view(A["w_out"][l])
                    for m in range(4):
                        sp_load(sp, main, st["B"] + 8 + m, 0, w[:, 2 * m:2 * m + 2, :], (2, D))
                elif k == "mix2":
                    w = cols_view(A["w_in_2"][l])
                    for m, (c0, cn) in enumerate(MIX2_COLS):
                        sp_load(sp, main, st["B"] + m, 0, w[:, :, c0:c0 + cn], (KD, cn))
                    w = rows_view(A["w_uq_2"][l])
                    sp_load(sp, main, st["B"] + 7, 0, w[:, 0:2, :], (2, NH * QK))
                    sp_load(sp, main, st["B"] + 8, 0, w[:, 2:3, :], (1, NH * QK))
                    sp_load(sp, main, st["B"] + 9, 0, rows_view(A["w_ukv_2"][l]), (2, D))
                    w = rows_view(A["w_out_2"][l])
                    for m in range(4):
                        sp_load(sp, main, st["B"] + 10 + m, 0, w[:, 2 * m:2 * m + 2, :], (2, D))
                elif k == "moe":
                    sp_experts(sp, main, st)
                    sp.wait_ge(ev("spill_known"), 1)
                    flag = sp.value_load(spill[0:1, 0:1])
                    with sp.If(flag > 0):
                        sp.wait_ge(main.lo_done, MOE_END)
                        sp.wait_ge(ev("spill_set"), 1)
                        sp_experts(sp, again, SPILL)
                        sp.wait_ge(again.added, 4 * NE)
                        sp.nop()
                    sp.end_ifs()
                elif k in ("ffn1", "ffn2a", "ffn2b"):
                    wg, wu, wd = weights_of(st)
                    sp_ffn(sp, main, st["B"], st["n"], cols_view(wg), cols_view(wu), rows_view(wd))
            sp.wait_ge(x_done, len(stages))
            sp.dma_start(out.rearrange("b (t p) d -> p (b t) d", p=P), x[:]).then_inc(stored, 16)
            sp.wait_ge(stored, 16)

        def act_hi(act, S, c, i, n=PIECE, free=()):
            act.wait_ge(S.raw_full[c % RING], 16 * (c // RING + 1 + i))
            for s, v in free:
                act.wait_ge(s, v)
            nc.scalar.copy(hi[:, c % RING, 0:n], raw[:, c % RING, 0:n]).then_inc(S.hi_done, 1)

        def act_static(act, n, size=PIECE):
            act_hi(act, main, n, 0, size, [done_of(n - RING)] if n >= RING else [])

        def act_ffn(act, S, st, w, i0=0):
            B, n, S0, R = st["B"], st["n"], st["S"] + i0, st["R"] + i0

            def silu(j):
                act.wait_ge(S.done["gate"], S0 + j + 1)
                act.wait_ge(S.hf_done, S0 + j)
                nc.scalar.activation(sg[:, :, 0:w], gate_ps(w), ACT.Silu).then_inc(S.sg_done, 1)

            def round_h(j):
                act.wait_ge(S.hf_done, S0 + j + 1)
                act.wait_ge(S.done["rows"], R + j)
                nc.scalar.copy(hh[:, :, 0:w], hf[:, :, 0:w]).then_inc(S.hh_done, 1)

            act_hi(act, S, B, i0, free=[(S.done["rows"], R - 1)])
            act_hi(act, S, B + 1, i0, free=[(S.done["rows"], R - 1)])
            with act.Fori(1, n) as j:
                act_hi(act, S, B - 1, i0 + j, free=[(S.done["gate"], S0 + j)])
                silu(j - 1)
                act_hi(act, S, B, i0 + j, free=[(S.done["up"], S0 + j)])
                round_h(j - 1)
                act_hi(act, S, B + 1, i0 + j, free=[(S.done["rows"], R + j - 1)])
            silu(n - 1)
            round_h(n - 1)
            act_hi(act, S, B + 3 * n - 1, i0, free=[(S.done["rows"], R + n - 1)])

        def act_stats(act, st):
            q = st["Q"]
            act.wait_ge(x_loaded, 16)
            act.wait_ge(x_done, q)
            for t in range(TT):
                nc.scalar.activation(xn[:, t, :], x[:, t, :], ACT.Square,
                                     accum_out=ssq[:, t:t + 1]).then_inc(ssq_done, 1)
            act.wait_ge(var_done, q + 1)
            nc.scalar.activation(std[:, 0:TT], var[:, 0:TT], ACT.Sqrt).then_inc(std_done, 1)

        def act_turned(act, st):
            for k in range(KD):
                act.wait_ge(turned, 4 * st["M"] + k // 2 + 1)
                nc.scalar.activation(xh[:, k, :], bank[DOWN[k // 2]][:, k % 2 * T:(k % 2 + 1) * T], ACT.Copy,
                                     scale=gain_of(st, k)).then_inc(xh_done, 1)

        def act_experts(act, S, st):
            nc.scalar.preload_act_table(ACT.Silu)
            with act.Fori(0, NE) as e:
                act.wait_ge(S.gathered, 2 * e + 1)
                for b in range(2):
                    nc.scalar.copy(xh[:, 4 * b:4 * b + 4, 0:P],
                                   bank[6 + b][:, :].rearrange("p (k s) -> p k s", k=4)).then_inc(S.gh_done, 1)
                act_ffn(act, S, st, P, STEPS1 * e)
                act.wait_ge(S.pick_turned, e + 1)
                nc.scalar.copy(pickT[:, :], bank[6][:, 0:T]).then_inc(S.pickT_done, 1)
                act.wait_ge(S.done["rows"], st["R"] + STEPS1 * (e + 1))
                for b in range(2):
                    nc.scalar.copy(yh[:, 512 * b:512 * b + 512], bank[2 + b][:, :]).then_inc(S.yh_done, 1)

        def act_mix1(act, st):
            B, C, l = st["B"], st["C"], st["layer"]
            for m in range(6):
                act_static(act, B + m)
            act.wait_ge(main.done["cols"], C + 3)
            act.wait_ge(ev("pads"), l + 1)
            nc.scalar.copy(apad[:, :, PAD:], bank[6][:, :].rearrange("p (c t) -> p c t", c=2)).then_inc(ev("a_out"), 1)
            act_static(act, B + 6)
            act.wait_ge(main.done["cols"], C + 4)
            nc.scalar.copy(gcT[:, :, :], bank[7][:, :].rearrange("p (c t) -> p c t", c=2)).then_inc(ev("gc_out"), 1)
            act.wait_ge(ev("v_var"), l + 1)
            nc.scalar.activation(std[:, 2:4], var[:, 2:4], ACT.Sqrt).then_inc(ev("v_std"), 1)
            act_static(act, B + 7)
            act_static(act, B + 8)
            act.wait_ge(main.done["cols"], C + 6)
            nc.scalar.copy(gb[:, :, :], bank[3][:, :].rearrange("p (t c) -> p t c", t=2)).then_inc(ev("gb_out"), 1)
            for i in range(2):
                act_static(act, B + 9 + i)
                act.wait_ge(main.done["cols"], C + 7 + i)
                nc.scalar.copy(u1[:, :, i * 256:i * 256 + 256],
                               bank[4 + i][:, :].rearrange("p (t c) -> p t c", t=2)).then_inc(ev("u_out"), 1)
            act.wait_ge(ev("y_raw"), l + 1)
            for t in range(TT):
                for g, (c0, c1) in enumerate(((0, DP), (DP, DP + DS), (DP + DS, D))):
                    nc.scalar.activation(xn[:, t, c0:c1], y1[:, t, c0:c1], ACT.Square,
                                         accum_out=ssq[:, 2 + 3 * t + g:3 + 3 * t + g]).then_inc(ev("y_sq"), 1)
            act.wait_ge(ev("y_var"), l + 1)
            nc.scalar.activation(std[:, 2:8], var[:, 2:8], ACT.Sqrt).then_inc(ev("y_std"), 1)
            nc.scalar.preload_act_table(ACT.Silu)
            for k in range(KD):
                act.wait_ge(ev("y_turned"), 4 * l + k // 2 + 1)
                nc.scalar.activation(xh[:, k, :], bank[Y_BANKS[k // 2]][:, k % 2 * T:(k % 2 + 1) * T], ACT.Copy,
                                     scale=col(("group", l), k)).then_inc(ev("yh_out"), 1)
            act_static(act, B + 11)

        def act_mix2(act, st):
            B, C, l = st["B"], st["C"], st["layer"]
            for m in range(4):
                act_static(act, B + m, KD * MIX2_COLS[m][1])
            for m in range(3):
                c0, cn = MIX2_COLS[m]
                act.wait_ge(main.done["cols"], C + m + 1)
                nc.scalar.copy(ptok[:, :, c0:c0 + cn], bank[MIX2_BANKS[m]][:, :].rearrange(
                    "p (t c) -> p t c", t=2)[:, :, 0:cn]).then_inc(ev("ptok_out"), 1)
                act_static(act, B + 4 + m)
            for t in range(TT):
                for g, (c0, c1) in enumerate(((0, QL), (QL, QL + KVL))):
                    act.wait_ge(ev("ptok_out"), 3 * (l + 1))
                    nc.scalar.activation(xn[:, t, c0:c1], ptok[:, t, c0:c1], ACT.Square,
                                         accum_out=ssq[:, 2 + 2 * t + g:3 + 2 * t + g]).then_inc(ev("lat_sq"), 1)
            act.wait_ge(ev("lat_var"), l + 1)
            nc.scalar.activation(std[:, 2:6], var[:, 2:6], ACT.Sqrt).then_inc(ev("lat_std"), 1)
            act_static(act, B + 7, 2 * NH * QK)
            for i in range(2):
                act.wait_ge(main.done["cols"], C + 6 + i)
                nc.scalar.activation(acc[:, 2 * i:2 * i + 2, :], bank[3 + i][:, :].rearrange("p (c t) -> p c t", c=2),
                                     ACT.Sigmoid).then_inc(ev("sig_out"), 1)
            act_static(act, B + 8, NH * QK)
            act_static(act, B + 9)
            for c in range(5):
                act.wait_ge(ev("lat_turned"), 3 * l + c // 2 + 1)
                g = col(("ql", l), c) if c < 3 else col(("kvl", l), c - 3)
                nc.scalar.activation(xh[:, c, :], bank[(5, 0, 1)[c // 2]][:, c % 2 * T:(c % 2 + 1) * T], ACT.Copy,
                                     scale=g).then_inc(ev("lath_out"), 1)
            act.wait_ge(main.done["cols"], C + 9)
            for t in range(TT):
                for h in range(2):
                    nc.scalar.copy(qk[:, t, 4 * h:4 * h + 4, :], bank[Q_BANKS[t][h]][:, 0:4 * QK].rearrange(
                        "p (h d) -> p h d", h=4)).then_inc(ev("q_out"), 1)
            act_static(act, B + 10)
            act_static(act, B + 11)
            act_static(act, B + 12)
            act.wait_ge(ev("q_out"), 4 * (l + 1))
            act.wait_ge(ev("k_out"), l + 1)
            nc.scalar.activation(sq2[:], qk[:], ACT.Square).then_inc(ev("qk_sq"), 1)
            act.wait_ge(ev("qk_var"), l + 1)
            nc.scalar.activation(hstd[:, :], hvar[:, :], ACT.Sqrt).then_inc(ev("qk_std"), 1)
            nc.scalar.preload_act_table(ACT.Exp)
            for g in range(8):
                act.wait_ge(ev("qk_turned"), 8 * l + g + 1)
                nc.scalar.copy(qkT[0:QK, 2 * g:2 * g + 2, :], bank[TURN4[g % 4]][0:QK, :].rearrange(
                    "p (h t) -> p h t", h=2)).then_inc(ev("qkT_out"), 1)
            for h in range(NH):
                act.wait_ge(ev("neg_max"), 8 * l + h + 1)
                if h >= 2:
                    act.wait_ge(ev("prob_turned"), 8 * l + h - 1)
                for t in range(TT):
                    c0, c1 = (0, P) if t == 0 else (P, 3 * P)
                    nc.scalar.activation(prob[:, h % 2, c0:c1], bank[h % 2][:, c0:c1], ACT.Exp,
                                         bias=negm[:, 2 * h + t:2 * h + t + 1], scale=SCALE,
                                         accum_out=psum_p[:, t * NH + h:t * NH + h + 1]).then_inc(ev("exp_out"), 1)
            act.wait_ge(ev("c_var"), l + 1)
            nc.scalar.activation(std[:, 2:4], var[:, 2:4], ACT.Sqrt).then_inc(ev("c_std"), 1)
            nc.scalar.preload_act_table(ACT.Silu)
            for b in range(2):
                act.wait_ge(ev("cat_turned"), 4 * l + b + 1)
                nc.scalar.copy(xh[:, 2 * b:2 * b + 2, :], bank[CAT_BANKS[b]][:, :].rearrange(
                    "p (c t) -> p c t", c=2)).then_inc(ev("cath_out"), 1)
            for c in range(4):
                act.wait_ge(ev("cat_turned"), 4 * l + 3 + c // 2)
                nc.scalar.activation(acc[:, c, :], bank[CAT_BANKS[2 + c // 2]][:, c % 2 * T:(c % 2 + 1) * T],
                                     ACT.Silu, scale=col(("clg", l), c), bias=col(("clb", l), c)).then_inc(achain, 1)
            act.wait_ge(achain, 4 * (l + 1))
            nc.scalar.copy(xh[:, 4:8, :], acc[:, :, :]).then_inc(ev("cath_out"), 1)
            act_static(act, B + 13)

        @block.scalar
        def _(act):
            act.dma_start(x[:], A["x"].rearrange("b (t p) d -> p (b t) d", p=P)).then_inc(x_loaded, 16)
            for tile, at, n, ap in staged:
                act.dma_start(stage_rows[at:at + n, tile, :], ap).then_inc(ev("rows_in"), 16)
            act.dma_start(stage_ws[:], A["sgu_w"].rearrange("l h i j -> i l h j")).then_inc(ev("ws_in"), 16)
            small = [
                (ropet[:], rope.rearrange("(t p) c -> p t c", p=P)),
                (vecs[:, 0, :], A["norm2_g"][1].partition_broadcast(P)),
                (vecs[:, 1, :], A["final_g"].partition_broadcast(P)),
                (vecs[:, 2, :], A["post_norm_2"][0].partition_broadcast(P)),
                (lng[:], A["sgu_ln_g"][0].partition_broadcast(P)),
                (lnb[:], A["sgu_ln_b"][0].partition_broadcast(P)),
                (psc[:], A["pool_scale"][0].partition_broadcast(P)),
                (qkg[:, :, 0, :], A["q_norm_2"].partition_broadcast(P)),
                (qkg[:, :, 1, :], A["k_norm_2"].partition_broadcast(P)),
                (routw[:], A["router_w"][0].rearrange("(k p) e -> p k e", p=P)),
                (routb[:], A["router_b"][0].partition_broadcast(P)),
            ]
            assert len(small) == N_SMALL
            for dst, src in small:
                act.dma_start(dst, src).then_inc(ev("small_in"), 16)
            act.wait_ge(ev("poolw_zero"), 1)
            for r in range(2):
                for l in range(2):
                    act.dma_start(poolw[64 * r:64 * r + 64, l, :, 64 * r:64 * r + 64],
                                  A["pool_w"][l, r::2].rearrange("c i o -> i c o")).then_inc(ev("poolw_in"), 16)
            for st in stages:
                k = st["kind"]
                act_stats(act, st)
                if k == "post":
                    continue
                if k in ("ffn1", "ffn2a", "ffn2b"):
                    nc.scalar.preload_act_table(ACT.Silu)
                if st["M"] == 0:
                    act.wait_ge(ev("chan_out"), 4)
                act_turned(act, st)
                if k == "mix1":
                    act_mix1(act, st)
                elif k == "mix2":
                    act_mix2(act, st)
                elif k == "moe":
                    act.wait_ge(ev("small_in"), 16 * N_SMALL)
                    nc.scalar.copy(rwh[:], routw[:]).then_inc(ev("rwh_out"), 1)
                    act.wait_ge(ev("h2_out"), 2)
                    for t in range(TT):
                        nc.scalar.copy(h2h[:, t, :], xn[:, t, :]).then_inc(ev("h2h_out"), 1)
                    act.wait_ge(ev("shifted"), 1)
                    nc.scalar.activation(ex[:], ex[:], ACT.Exp).then_inc(ev("ex_out"), 1)
                    act_experts(act, main, st)
                    act.wait_ge(ev("spill_known"), 1)
                    flag = act.value_load(spill[0:1, 0:1])
                    with act.If(flag > 0):
                        act.wait_ge(main.added, 4 * NE)
                        act.wait_ge(ev("spill_set"), 1)
                        act_experts(act, again, SPILL)
                        act.wait_ge(again.added, 4 * NE)
                        act.nop()
                    act.end_ifs()
                else:
                    act_ffn(act, main, st, T)

        def pe_cols(pe, S, c, i, bk, w, free=()):
            pe.wait_ge(S.lo_done, c + 1 + 3 * i)
            for s, v in free:
                pe.wait_ge(s, v)
            r = c % RING
            for s in range(2):
                o = bank[bk][:, s * w:(s + 1) * w]
                for k in range(KD):
                    a = k * FW + s * P
                    pe.matmul(o, hi[:, r, a:a + P], xh[:, k, 0:w], start=(k == 0), stop=False)
                    pe.matmul(o, hi[:, r, a:a + P], xl[:, k, 0:w], start=False, stop=False)
                    mm = pe.matmul(o, lo[:, r, a:a + P], xh[:, k, 0:w], start=False, stop=(k == KD - 1))
            return mm

        def pe_toks(pe, c, bk, cn, ks=range(KD), x0=0, out0=0, stride=256, first=True, last=True, c0=0, row=None):
            r, row = c % RING, row or cn
            for t in range(TT):
                o = bank[bk[t]][:, t * stride:t * stride + cn]
                for n, k in enumerate(ks):
                    wgt = slice(n * row + c0, n * row + c0 + cn)
                    tk = slice(t * P, t * P + P)
                    pe.matmul(o, xh[:, x0 + k, tk], hi[:, r, wgt], start=(first and n == 0), stop=False)
                    pe.matmul(o, xh[:, x0 + k, tk], lo[:, r, wgt], start=False, stop=False)
                    mm = pe.matmul(o, xl[:, x0 + k, tk], hi[:, r, wgt], start=False, stop=(last and n == len(ks) - 1))
            return mm

        def pe_rows(pe, S, c, i, ah, al, nt, first=False, last=False):
            pe.wait_ge(S.lo_done, c + 1 + 3 * i)
            r = c % RING
            for s in range(2):
                for t in range(nt):
                    tk = slice(t * P, t * P + P)
                    for h in range(2):
                        o = bank[DOWN[2 * t + h]][:, :]
                        wgt = slice(s * D + h * 512, s * D + h * 512 + 512)
                        pe.matmul(o, ah[:, s, tk], hi[:, r, wgt], start=(first and s == 0), stop=False,
                                  skip_group_check=True)
                        pe.matmul(o, ah[:, s, tk], lo[:, r, wgt], start=False, stop=False, skip_group_check=True)
                    for h in range(2):
                        o = bank[DOWN[2 * t + h]][:, :]
                        wgt = slice(s * D + h * 512, s * D + h * 512 + 512)
                        mm = pe.matmul(o, al[:, s, tk], hi[:, r, wgt], start=False, stop=(last and s == 1),
                                       skip_group_check=True)
            return mm.then_inc(S.done["rows"], 1)

        def pe_ffn(pe, S, st, w, i0=0):
            B, n, S0 = st["B"], st["n"], st["S"] + i0
            nt = w // P

            def open_down():
                for b in range(2 * nt):
                    pe.matmul(bank[DOWN[b]][:, :], zeros[:, 0:P], zeros[:, :], start=True, stop=False,
                              skip_group_check=True)

            def gate(c, i, j):
                pe_cols(pe, S, c, i, GATE, w, [(S.sg_done, S0 + j)]).then_inc(S.done["gate"], 1)

            def up(c, i, j):
                pe_cols(pe, S, c, i, UP, w, [(S.hf_done, S0 + j)]).then_inc(S.done["up"], 1)

            open_down()
            gate(B, i0, 0)
            up(B + 1, i0, 0)
            with pe.Fori(1, n) as j:
                gate(B - 1, i0 + j, j)
                up(B, i0 + j, j)
                pe.wait_ge(S.hl_done, S0 + j)
                pe_rows(pe, S, B + 1, i0 + j, hh, hl, nt)
            pe.wait_ge(S.hl_done, S0 + n)
            pe_rows(pe, S, B + 3 * n - 1, i0, hh, hl, nt, last=True)

        def pe_turn(pe, src, banks, chunks, signal):
            for k in chunks:
                for t in range(TT):
                    o = bank[banks[k // 2]][:, k % 2 * T + t * P:k % 2 * T + t * P + P]
                    mm = pe.transpose(o, src[:, t, k * P:k * P + P], ident[:, :])
                if k % 2 or k == chunks[-1]:
                    mm.then_inc(signal, 1)

        def pe_experts(pe, S, st):
            with pe.Fori(0, NE) as e:
                pe.wait_ge(S.pick_done, 2 * e + 2)
                pe.wait_ge(S.added, 4 * e)
                for src, b0 in ((h2h, 6), (h2l, 4)):
                    for k in range(KD):
                        o = bank[b0 + k // 4][:, k % 4 * P:k % 4 * P + P]
                        for t in range(TT):
                            mm = pe.matmul(o, src[:, t, k * P:k * P + P], pick[:, t, :], start=(t == 0), stop=(t == 1))
                    mm.then_inc(S.gathered, 1)
                pe.wait_ge(S.yl_done, 2 * e)
                pe.wait_ge(S.gh_done, 2 * e + 2)
                pe.wait_ge(S.gl_done, 2 * e + 2)
                for t in range(TT):
                    mm = pe.transpose(bank[6][:, t * P:t * P + P], pick[:, t, :].bitcast(F32), ident[:, :])
                mm.then_inc(S.pick_turned, 1)
                pe_ffn(pe, S, st, P, STEPS1 * e)
                pe.wait_ge(S.pickT_done, e + 1)
                pe.wait_ge(S.yh_done, 2 * e + 2)
                pe.wait_ge(S.yl_done, 2 * e + 2)
                for t in range(TT):
                    for h in range(2):
                        o = bank[4 + 2 * t + h][:, :]
                        pe.matmul(o, pickT[:, t * P:t * P + P], yh[:, h * 512:h * 512 + 512], start=True, stop=False)
                        pe.matmul(o, pickT[:, t * P:t * P + P], yl[:, h * 512:h * 512 + 512], start=False,
                                  stop=True).then_inc(S.spread, 1)

        def pe_mix1(pe, st):
            B, l = st["B"], st["layer"]
            for m in range(8):
                n, bk = B + m, MIX1_BANKS[m]
                if m in (2, 3, 4):
                    pe_cols(pe, main, n, 0, bk, T).then_inc(main.done["cols"], 1)
                else:
                    pe.wait_ge(main.lo_done, n + 1)
                    pe_toks(pe, n, (bk, bk), FW).then_inc(main.done["cols"], 1)
            pe.wait_ge(ev("vn_out"), 2 * (l + 1))
            for t in range(TT):
                for h in range(SH):
                    mm = pe.matmul(bank[t][:, h * P:h * P + P], wsT[:, l, h, :], vn[:, t, h * P:h * P + P],
                                   start=True, stop=True)
                mm.then_inc(ev("sgu_out"), 1)
            pe.wait_ge(ev("pool_in"), l + 1)
            pe.wait_ge(ev("poolw_in"), 64)
            for t in range(TT):
                for c in range(2):
                    mm = pe.matmul(bank[6][:, t * 256 + c * P:t * 256 + c * P + P], dT[:, c, t * P:t * P + P],
                                   poolw[:, l, c, :], start=True, stop=True)
            mm.then_inc(ev("pool_out"), 1)
            pe.wait_ge(ev("conv_in"), l + 1)
            for t in range(TT):
                for c in range(2):
                    mm = pe.transpose(bank[7][:, t * 256 + c * P:t * 256 + c * P + P], zc[:, c, t * P:t * P + P],
                                      ident[:, :])
            mm.then_inc(ev("conv_out"), 1)
            pe.wait_ge(ev("y_ready"), l + 1)
            pe_turn(pe, y1, Y_BANKS, range(KD), ev("y_turned"))
            pe.wait_ge(ev("yl_out"), 8 * (l + 1))
            for m in range(4):
                pe_rows(pe, main, B + 8 + m, 0, xh[:, 2 * m:2 * m + 2, :], xl[:, 2 * m:2 * m + 2, :], TT,
                        first=(m == 0), last=(m == 3))

        def pe_mix2(pe, st):
            B, l = st["B"], st["layer"]
            for m in range(7):
                n, bk = B + m, MIX2_BANKS[m]
                if m >= 3:
                    pe_cols(pe, main, n, 0, bk, T).then_inc(main.done["cols"], 1)
                else:
                    pe.wait_ge(main.lo_done, n + 1)
                    pe_toks(pe, n, (bk, bk), MIX2_COLS[m][1]).then_inc(main.done["cols"], 1)
            pe.wait_ge(ev("lat_ready"), l + 1)
            pe_turn(pe, ptok, (5, 0, 1), range(5), ev("lat_turned"))
            pe.wait_ge(ev("latl_out"), 5 * (l + 1))
            pe.wait_ge(ev("u_ready"), l + 1)
            for m, ks in ((7, (0, 1)), (8, (2,))):
                pe.wait_ge(main.lo_done, B + m + 1)
                for h in range(2):
                    mm = pe_toks(pe, B + m, (Q_BANKS[0][h], Q_BANKS[1][h]), 4 * QK, ks, stride=0, first=(m == 7),
                                 last=(m == 8), c0=h * 4 * QK, row=NH * QK)
                mm.then_inc(main.done["cols"], 1)
            pe.wait_ge(main.lo_done, B + 10)
            for h in range(2):
                mm = pe_toks(pe, B + 9, (KV_BANKS[0][h], KV_BANKS[1][h]), 512, (3, 4), stride=0, c0=h * 512, row=D)
            mm.then_inc(main.done["cols"], 1)
            pe.wait_ge(ev("qk_ready"), l + 1)
            for g in range(8):
                if g >= 4:
                    pe.wait_ge(ev("qkT_out"), 8 * l + g - 3)
                for h in range(2):
                    for t in range(TT):
                        mm = pe.transpose(bank[TURN4[g % 4]][0:QK, h * T + t * P:h * T + t * P + P],
                                          qk[:, t, 2 * g + h, :], ident[:, :])
                mm.then_inc(ev("qk_turned"), 1)
            pe.wait_ge(ev("qkT_out"), 8 * (l + 1))
            for i in range(NH + 2):
                if i < NH:
                    h = i
                    if h >= 2:
                        pe.wait_ge(ev("exp_out"), 16 * l + 2 * (h - 1))
                    pe.matmul(bank[h % 2][:, 0:P], qkT[0:QK, h, 0:P], qkT[0:QK, NH + h, 0:P], start=True, stop=True)
                    pe.matmul(bank[h % 2][:, P:3 * P], qkT[0:QK, h, P:T], qkT[0:QK, NH + h, :], start=True,
                              stop=True).then_inc(ev("score_out"), 1)
                if 1 <= i <= NH:
                    h = i - 1
                    pe.wait_ge(ev("exp_out"), 16 * l + 2 * (h + 1))
                    if h >= 2:
                        pe.wait_ge(ev("probT_out"), 8 * l + h - 1)
                    for b in range(3):
                        mm = pe.transpose(bank[4 + h % 2][:, b * P:b * P + P], prob[:, h % 2, b * P:b * P + P],
                                          ident[:, :])
                    mm.then_inc(ev("prob_turned"), 1)
                if i >= 2:
                    h = i - 2
                    pe.wait_ge(ev("probT_out"), 8 * l + h + 1)
                    pe.matmul(bank[6][:, h * VD:h * VD + VD], probT[:, h % 2, 0:P], v2[:, 0, h, :], start=True,
                              stop=True)
                    pe.matmul(bank[7][:, h * VD:h * VD + VD], probT[:, h % 2, P:T], v2[:, 0, h, :], start=True,
                              stop=False)
                    pe.matmul(bank[7][:, h * VD:h * VD + VD], probT[:, h % 2, T:3 * P], v2[:, 1, h, :], start=False,
                              stop=True).then_inc(ev("att_out"), 1)
            pe.wait_ge(ev("conv31_out"), l + 1)
            for t in range(TT):
                for c in range(4):
                    mm = pe.transpose(bank[2 + t][:, c * P:c * P + P], acc[:, c, t * P:t * P + P], ident[:, :])
            mm.then_inc(ev("c_turned"), 1)
            pe.wait_ge(ev("att_ready"), l + 1)
            pe_turn(pe, xn, CAT_BANKS, range(4), ev("cat_turned"))
            pe.wait_ge(ev("c_ready"), l + 1)
            pe_turn(pe, xn, CAT_BANKS, range(4, 8), ev("cat_turned"))
            pe.wait_ge(ev("catl_out"), 3 * (l + 1))
            for m in range(4):
                pe_rows(pe, main, B + 10 + m, 0, xh[:, 2 * m:2 * m + 2, :], xl[:, 2 * m:2 * m + 2, :], TT,
                        first=(m == 0), last=(m == 3))

        def pe_router(pe):
            pe.wait_ge(ev("rwl_out"), 1)
            for t in range(TT):
                for k in range(KD):
                    for n, (a, b) in enumerate(((xh, rwh), (xh, rwl), (xl, rwh), (xl, rwl))):
                        mm = pe.matmul(bank[6][:, t * NE:t * NE + NE], a[:, k, t * P:t * P + P], b[:, k, :],
                                       start=(k == 0 and n == 0), stop=(k == KD - 1 and n == 3))
            mm.then_inc(ev("logit_out"), 1)
            pe.wait_ge(ev("sel_out"), 1)
            pe.matmul(bank[7][:, 0:NE], before[:, :], sel[:, 0, :], start=True, stop=True)
            pe.matmul(bank[7][:, NE:2 * NE], ones[:, :], sel[:, 0, :], start=True, stop=False)
            pe.matmul(bank[7][:, NE:2 * NE], before[:, :], sel[:, 1, :], start=False, stop=True)
            pe.matmul(bank[7][:, 2 * NE:3 * NE], ones[:, :], sel[:, 0, :], start=True, stop=False)
            pe.matmul(bank[7][:, 2 * NE:3 * NE], ones[:, :], sel[:, 1, :], start=False, stop=True)\
              .then_inc(ev("count_out"), 1)

        @block.tensor
        def _(pe):
            pe.wait_ge(ev("const_pool"), N_POOL)
            pe.wait_ge(ev("rows_in"), 16 * len(staged))
            for tile in range(4):
                n = used[tile]
                pe.transpose(bank[tile][:, 0:n], stage_rows[0:n, tile, :], ident[0:n, 0:n]).then_inc(ev("chan_turned"), 1)
            pe.wait_ge(ev("ws_in"), 16)
            for l in range(2):
                for h in range(SH):
                    mm = pe.transpose(bank[4 + l][:, h * P:h * P + P], stage_ws[:, l, h, :], ident[:, :])
                mm.then_inc(ev("ws_turned"), 1)
            pe.wait_ge(ev("const_vec"), N_VEC)
            pe.wait_ge(ev("chan_out"), 4)
            for st in stages:
                k = st["kind"]
                if k == "post":
                    continue
                pe.wait_ge(xn_done, TT * (st["M"] + 1))
                pe_turn(pe, xn, DOWN, range(KD), turned)
                pe.wait_ge(xl_done, KD * (st["M"] + 1))
                if k == "mix1":
                    pe_mix1(pe, st)
                elif k == "mix2":
                    pe_mix2(pe, st)
                elif k == "moe":
                    pe_router(pe)
                    pe.wait_ge(ev("h2l_out"), 2)
                    pe_experts(pe, main, st)
                    pe.wait_ge(ev("spill_known"), 1)
                    flag = pe.value_load(spill[0:1, 0:1])
                    with pe.If(flag > 0):
                        pe.wait_ge(main.added, 4 * NE)
                        pe.wait_ge(ev("spill_set"), 1)
                        pe_experts(pe, again, SPILL)
                        pe.wait_ge(again.added, 4 * NE)
                        pe.nop()
                    pe.end_ifs()
                else:
                    pe_ffn(pe, main, st, T)

        @block.gpsimd
        def _(pool):
            g = nc.gpsimd
            n = 0

            def link(ins):
                nonlocal n
                n += 1
                ins.then_inc(pchain, 1)
                pool.wait_ge(pchain, n)

            link(g.memset(poolw[:], 0.0))
            g.memset(ptouch[:], 0.0).then_inc(ev("poolw_zero"), 1)
            link(g.memset(ident[:], 0.0))
            link(g.memset(ones[:], 1.0))
            g.affine_select(out=ident[:], in_=ident[:], compare_op=ALU.not_equal, fill=1.0, base=0,
                            pattern=[[-1, P]], channel_multiplier=1).then_inc(ev("const_pool"), 1)
            g.affine_select(out=before[:], in_=ones[:], compare_op=ALU.is_gt, fill=0.0, base=0,
                            pattern=[[1, P]], channel_multiplier=-1).then_inc(ev("const_pool"), 1)
            g.iota(slots[:], pattern=[[1, P]], base=0, channel_multiplier=0,
                   allow_small_or_imprecise_dtypes=True).then_inc(ev("const_pool"), 1)
            g.iota(invc[:], pattern=[[0, 2], [1, T]], base=1, channel_multiplier=0,
                   allow_small_or_imprecise_dtypes=True).then_inc(ev("const_pool"), 1)
            g.affine_select(out=earlier[:], in_=ones[:, 0:NE * NE].rearrange("p (e j) -> p e j", e=NE),
                            compare_op=ALU.is_gt, fill=0.0, base=0, pattern=[[1, NE], [-1, NE]],
                            channel_multiplier=0).then_inc(ev("const_pool"), 1)
            pool.wait_ge(ev("y_raw"), 1)
            for dst, name in ((lng, "sgu_ln_g"), (lnb, "sgu_ln_b"), (psc, "pool_scale")):
                pool.dma_start(dst[:], A[name][1].partition_broadcast(P)).then_inc(ev("small1_in"), 16)
            pool.wait_ge(ev("h2_out"), 2)
            pool.dma_start(vecs[:, 0, :], A["post_norm_2"][1].partition_broadcast(P)).then_inc(ev("post1_in"), 16)

        @block.vector
        def _(dve):
            v = nc.vector
            count = [0]

            def note(ins):
                count[0] += 1
                ins.then_inc(chain, 1)

            def settle():
                dve.wait_ge(chain, count[0])

            def link(ins):
                note(ins)
                settle()

            marks = [0]

            def mark(s, inc=1):
                v.memset(touch[:, marks[0]:marks[0] + 1], 0.0).then_inc(s, inc)
                marks[0] += 1

            def lo_piece(S, c, i, n=PIECE):
                dve.wait_ge(S.hi_done, c + 1 + 3 * i)
                v.tensor_tensor(lo[:, c % RING, 0:n], raw[:, c % RING, 0:n], hi[:, c % RING, 0:n].bitcast(F32),
                                ALU.subtract).then_inc(S.lo_done, 1)

            def ffn(S, st, w, i0=0):
                B, n, S0 = st["B"], st["n"], st["S"] + i0

                def hidden(j):
                    dve.wait_ge(S.sg_done, S0 + j + 1)
                    dve.wait_ge(S.done["up"], S0 + j + 1)
                    dve.wait_ge(S.hl_done, S0 + j)
                    v.tensor_tensor(hf[:, :, 0:w], sg[:, :, 0:w], up_ps(w), ALU.mult).then_inc(S.hf_done, 1)

                def rest_h(j):
                    dve.wait_ge(S.hh_done, S0 + j + 1)
                    v.tensor_tensor(hl[:, :, 0:w], hf[:, :, 0:w], hh[:, :, 0:w].bitcast(F32),
                                    ALU.subtract).then_inc(S.hl_done, 1)

                lo_piece(S, B, i0)
                lo_piece(S, B + 1, i0)
                with dve.Fori(1, n) as j:
                    lo_piece(S, B - 1, i0 + j)
                    hidden(j - 1)
                    lo_piece(S, B, i0 + j)
                    rest_h(j - 1)
                    lo_piece(S, B + 1, i0 + j)
                hidden(n - 1)
                rest_h(n - 1)
                lo_piece(S, B + 3 * n - 1, i0)

            def stats(st):
                q = st["Q"]
                dve.wait_ge(ssq_done, TT * (q + 1))
                v.tensor_scalar(var[:, 0:TT], ssq[:, 0:TT], 1.0 / D, EPS, ALU.mult, ALU.add).then_inc(var_done, 1)
                dve.wait_ge(std_done, q + 1)
                link(v.reciprocal(rstd[:, 0:TT], std[:, 0:TT]))

            def add_down(factor, R):
                dve.wait_ge(main.done["rows"], R)
                for b in range(4):
                    xs = x[:, b // 2, b % 2 * 512:b % 2 * 512 + 512]
                    ins = v.scalar_tensor_tensor(xs, bank[DOWN[b]][:, :], factor, xs, ALU.mult, ALU.add)
                ins.then_inc(x_done, 1)

            def turned_rest(dst, src, gain, high, signal):
                v.scalar_tensor_tensor(dst, src, gain, high.bitcast(F32), ALU.mult, ALU.subtract).then_inc(signal, 1)

            def mix1(st):
                B, C, l = st["B"], st["C"], st["layer"]
                v.memset(apad[:, :, 0:PAD], 0.0).then_inc(ev("pads"), 1)
                link(v.memset(zpad[:, :, 0:CW - 1], 0.0))
                for m in range(5):
                    lo_piece(main, B + m, 0)
                dve.wait_ge(main.done["cols"], C + 2)
                for t in range(TT):
                    for b in range(2):
                        note(v.bn_stats(bns[:, t, b, :], bank[b][:, t * 256:t * 256 + 256]))
                settle()
                for t in range(TT):
                    note(v.bn_aggr(bna[:, t, :], bns[:, t, :, :]))
                settle()
                v.tensor_scalar(var[:, 2:4], bna[:, :, 1], EPS, None, ALU.add).then_inc(ev("v_var"), 1)
                lo_piece(main, B + 5, 0)
                lo_piece(main, B + 6, 0)
                dve.wait_ge(ev("v_std"), l + 1)
                link(v.reciprocal(rstd[:, 2:4], std[:, 2:4]))
                for t in range(TT):
                    for b in range(2):
                        note(v.tensor_scalar(vn[:, t, b * 256:b * 256 + 256], bank[b][:, t * 256:t * 256 + 256],
                                             bna[:, t, 0:1], rstd[:, 2 + t:3 + t], ALU.subtract, ALU.mult))
                settle()
                if l == 0:
                    dve.wait_ge(ev("small_in"), 16 * N_SMALL)
                else:
                    dve.wait_ge(ev("small1_in"), 48)
                for t in range(TT):
                    note(v.tensor_tensor(vn[:, t, :], vn[:, t, :], lng[:, :], ALU.mult))
                settle()
                for t in range(TT):
                    v.tensor_tensor(vn[:, t, :], vn[:, t, :], lnb[:, :], ALU.add).then_inc(ev("vn_out"), 1)
                lo_piece(main, B + 7, 0)
                dve.wait_ge(ev("a_out"), l + 1)
                N = PAD + T
                link(v.tensor_tensor(w2[:, :, 1:N], apad[:, :, 1:N], apad[:, :, 0:N - 1], ALU.add))
                link(v.tensor_tensor(w4[:, :, 3:N], w2[:, :, 3:N], w2[:, :, 1:N - 2], ALU.add))
                link(v.tensor_tensor(w8[:, 1, 7:N], w4[:, 1, 7:N], w4[:, 1, 3:N - 4], ALU.add))
                link(v.tensor_tensor(w16[:, 1, 15:N], w8[:, 1, 15:N], w8[:, 1, 7:N - 8], ALU.add))
                for g, wsum in enumerate((w2, w4, w8, w16)):
                    pr, c = slice(g % 2 * 64, g % 2 * 64 + 64), g // 2
                    note(v.tensor_tensor(dT[pr, c, :], wsum[pr, c, PAD:N], invc[pr, c, :], ALU.mult))
                settle()
                v.tensor_tensor(dT[:, :, :], dT[:, :, :], apad[:, :, PAD:N], ALU.subtract).then_inc(ev("pool_in"), 1)
                dve.wait_ge(ev("gc_out"), l + 1)
                dve.wait_ge(main.done["cols"], C + 5)
                link(v.tensor_tensor(zpad[:, :, CW - 1:], gcT[:, :, :], bank[2][:, :].rearrange(
                    "p (c t) -> p c t", c=2), ALU.mult))
                for c in range(2):
                    note(v.tensor_scalar(zc[:, c, :], zpad[:, c, 0:T], col(("cw", l), c), None, ALU.mult))
                settle()
                for k in range(1, CW):
                    for c in range(2):
                        ins = v.scalar_tensor_tensor(zc[:, c, :], zpad[:, c, k:k + T], col(("cw", l), 2 * k + c),
                                                     zc[:, c, :], ALU.mult, ALU.add)
                        note(ins)
                    settle()
                mark(ev("conv_in"))
                for m in range(8, 11):
                    lo_piece(main, B + m, 0)
                dve.wait_ge(ev("sgu_out"), 2 * (l + 1))
                dve.wait_ge(ev("u_out"), 2 * (l + 1))
                for t in range(TT):
                    for h in range(SH):
                        v.scalar_tensor_tensor(y1[:, t, DP + h * P:DP + h * P + P], bank[t][:, h * P:h * P + P],
                                               col(("sb", l), h), u1[:, t, h * P:h * P + P], ALU.add, ALU.mult)
                dve.wait_ge(ev("pool_out"), l + 1)
                for t in range(TT):
                    v.tensor_tensor(y1[:, t, 0:DP], bank[6][:, t * 256:t * 256 + 256], psc[:, :], ALU.mult)
                dve.wait_ge(ev("conv_out"), l + 1)
                dve.wait_ge(ev("gb_out"), l + 1)
                for t in range(TT):
                    ins = v.tensor_tensor(y1[:, t, DP + DS:D], gb[:, t, :], bank[7][:, t * 256:t * 256 + 256], ALU.mult)
                ins.then_inc(ev("y_raw"), 1)
                dve.wait_ge(ev("y_sq"), 6 * (l + 1))
                sums = ssq[:, 2:8].rearrange("p (t g) -> p t g", t=2)
                vars_ = var[:, 2:8].rearrange("p (t g) -> p t g", t=2)
                for g, n in enumerate((DP, DS, DC)):
                    ins = v.tensor_scalar(vars_[:, :, g], sums[:, :, g], 1.0 / n, EPS, ALU.mult, ALU.add)
                ins.then_inc(ev("y_var"), 1)
                dve.wait_ge(ev("y_std"), l + 1)
                link(v.reciprocal(rstd[:, 2:8], std[:, 2:8]))
                for t in range(TT):
                    for g, (c0, c1) in enumerate(((0, DP), (DP, DP + DS), (DP + DS, D))):
                        ins = v.tensor_scalar(y1[:, t, c0:c1], y1[:, t, c0:c1], rstd[:, 2 + 3 * t + g:3 + 3 * t + g],
                                              None, ALU.mult)
                ins.then_inc(ev("y_ready"), 1)
                for k in range(KD):
                    dve.wait_ge(ev("yh_out"), 8 * l + bank_end(k, KD))
                    turned_rest(xl[:, k, :], bank[Y_BANKS[k // 2]][:, k % 2 * T:(k % 2 + 1) * T],
                                col(("group", l), k), xh[:, k, :], ev("yl_out"))
                lo_piece(main, B + 11, 0)
                add_down(1.0, st["R"] + 4)

            def router(st):
                lo_router = v.tensor_tensor
                dve.wait_ge(ev("rwh_out"), 1)
                lo_router(rwl[:], routw[:], rwh[:].bitcast(F32), ALU.subtract).then_inc(ev("rwl_out"), 1)
                for t in range(TT):
                    v.tensor_tensor(xn[:, t, :], xn[:, t, :], vecs[:, 0, :], ALU.mult).then_inc(ev("h2_out"), 1)
                for t in range(TT):
                    dve.wait_ge(ev("h2h_out"), t + 1)
                    v.tensor_tensor(h2l[:, t, :], xn[:, t, :], h2h[:, t, :].bitcast(F32),
                                    ALU.subtract).then_inc(ev("h2l_out"), 1)
                dve.wait_ge(ev("logit_out"), 1)
                for t in range(TT):
                    note(v.tensor_tensor(logit[:, t, :], bank[6][:, t * NE:t * NE + NE], routb[:, :], ALU.add))
                settle()
                for t in range(TT):
                    mine = logit[:, t, :].unsqueeze(2).to_broadcast([P, NE, NE])
                    other = logit[:, t, :].unsqueeze(1).to_broadcast([P, NE, NE])
                    b1 = big[:, t, :].rearrange("p (e j) -> p e j", e=NE)
                    b2 = big2[:, t, :].rearrange("p (e j) -> p e j", e=NE)
                    note(v.tensor_tensor(b1, other, mine, ALU.is_gt))
                    note(v.tensor_tensor(b2, other, mine, ALU.is_equal))
                    settle()
                    link(v.tensor_tensor(b2, b2, earlier[:, :, :], ALU.mult))
                    link(v.tensor_tensor(b1, b1, b2, ALU.add))
                    note(v.tensor_reduce(place[:, t, :], b1, AX, ALU.add))
                    note(v.tensor_reduce(top[:, t:t + 1], logit[:, t, :], AX, ALU.max))
                settle()
                v.tensor_scalar(sel[:], place[:], float(2), None, ALU.is_lt).then_inc(ev("sel_out"), 1)
                for t in range(TT):
                    ins = v.tensor_scalar(ex[:, t, :], logit[:, t, :], top[:, t:t + 1], None, ALU.subtract)
                ins.then_inc(ev("shifted"), 1)
                dve.wait_ge(ev("ex_out"), 1)
                link(v.tensor_tensor(gates[:], ex[:], sel[:], ALU.mult))
                link(v.tensor_reduce(den[:, :], gates[:], AX, ALU.add))
                link(v.reciprocal(rden[:, :], den[:, :]))
                for t in range(TT):
                    note(v.tensor_scalar(gates[:, t, :], gates[:, t, :], rden[:, t:t + 1], None, ALU.mult))
                settle()
                dve.wait_ge(ev("count_out"), 1)
                note(v.memset(rank[:], -1.0))
                settle()
                for t in range(TT):
                    note(v.scalar_tensor_tensor(rank[:, t, 0, 0:NE], bank[7][:, t * NE:t * NE + NE], 1.0, sel[:, t, :],
                                                ALU.add, ALU.mult))
                note(v.tensor_reduce(most[:, :], bank[7][:, 2 * NE:3 * NE], AX, ALU.max))
                settle()
                for t in range(TT):
                    note(v.tensor_scalar(rank[:, t, 1, 0:NE], rank[:, t, 0, 0:NE], -1.0 - P, None, ALU.add))
                settle()
                for t in range(TT):
                    note(v.tensor_scalar(rank[:, t, 0, 0:NE], rank[:, t, 0, 0:NE], -1.0, None, ALU.add))
                settle()
                v.tensor_scalar(spill[0:1, 0:1], most[0:1, 0:1], float(P), None, ALU.is_gt).then_inc(ev("spill_known"), 1)

            def pick_of(S, pass_, e):
                for t in range(TT):
                    v.tensor_scalar(pick[:, t, :], slots[:, :], rank[:, t, pass_, bass.ds(e, 1)], None,
                                    ALU.is_equal).then_inc(S.pick_done, 1)

            def experts(S, st, pass_):
                pick_of(S, pass_, 0)
                with dve.Fori(0, NE) as e:
                    dve.wait_ge(S.gathered, 2 * e + 2)
                    for b in range(2):
                        v.tensor_copy(xl[:, 4 * b:4 * b + 4, 0:P], bank[4 + b][:, :].rearrange(
                            "p (k s) -> p k s", k=4)).then_inc(S.gl_done, 1)
                    ffn(S, st, P, STEPS1 * e)
                    dve.wait_ge(S.pick_turned, e + 1)
                    pick_of(S, pass_, e + 1)
                    for b in range(2):
                        dve.wait_ge(S.yh_done, 2 * e + b + 1)
                        v.tensor_tensor(yl[:, 512 * b:512 * b + 512], bank[2 + b][:, :],
                                        yh[:, 512 * b:512 * b + 512].bitcast(F32), ALU.subtract).then_inc(S.yl_done, 1)
                    for b in range(4):
                        dve.wait_ge(S.spread, 4 * e + b + 1)
                        xs = x[:, b // 2, b % 2 * 512:b % 2 * 512 + 512]
                        v.scalar_tensor_tensor(xs, bank[4 + b][:, :], gates[:, b // 2, bass.ds(e, 1)], xs, ALU.mult,
                                               ALU.add).then_inc(S.added, 1)

            def mix2(st):
                B, C, l = st["B"], st["C"], st["layer"]
                link(v.memset(upad[:, :, 0:CPAD], 0.0))
                for m in range(7):
                    lo_piece(main, B + m, 0, KD * MIX2_COLS[m][1])
                dve.wait_ge(ev("lat_sq"), 4 * (l + 1))
                sums = ssq[:, 2:6].rearrange("p (t g) -> p t g", t=2)
                vars_ = var[:, 2:6].rearrange("p (t g) -> p t g", t=2)
                for g, n in enumerate((QL, KVL)):
                    ins = v.tensor_scalar(vars_[:, :, g], sums[:, :, g], 1.0 / n, EPS, ALU.mult, ALU.add)
                ins.then_inc(ev("lat_var"), 1)
                dve.wait_ge(ev("lat_std"), l + 1)
                link(v.reciprocal(rstd[:, 2:6], std[:, 2:6]))
                for t in range(TT):
                    for g, (c0, c1) in enumerate(((0, QL), (QL, QL + KVL))):
                        ins = v.tensor_scalar(ptok[:, t, c0:c1], ptok[:, t, c0:c1], rstd[:, 2 + 2 * t + g:3 + 2 * t + g],
                                              None, ALU.mult)
                ins.then_inc(ev("lat_ready"), 1)
                lo_piece(main, B + 7, 0, 2 * NH * QK)
                for i in range(2):
                    dve.wait_ge(ev("sig_out"), 2 * l + i + 1)
                    ins = v.tensor_tensor(upad[:, 2 * i:2 * i + 2, CPAD:], acc[:, 2 * i:2 * i + 2, :],
                                          bank[(7, 2)[i]][:, :].rearrange("p (c t) -> p c t", c=2), ALU.mult)
                ins.then_inc(ev("u_ready"), 1)
                lo_piece(main, B + 8, 0, NH * QK)
                lo_piece(main, B + 9, 0)
                for c in range(5):
                    dve.wait_ge(ev("lath_out"), 5 * l + bank_end(c, 5))
                    g = col(("ql", l), c) if c < 3 else col(("kvl", l), c - 3)
                    turned_rest(xl[:, c, :], bank[(5, 0, 1)[c // 2]][:, c % 2 * T:(c % 2 + 1) * T], g, xh[:, c, :],
                                ev("latl_out"))
                taps = [(k, c) for k in range(CK) for c in range(4)]

                def conv(n):
                    for _ in range(n):
                        if not taps:
                            return
                        k, c = taps.pop(0)
                        w = col(("cw2", l), 4 * k + c)
                        if k == 0:
                            if c == 0:
                                dve.wait_ge(ev("u_ready"), l + 1)
                            note(v.tensor_scalar(acc[:, c, :], upad[:, c, 0:T], w, col(("cb", l), c), ALU.mult, ALU.add))
                        else:
                            dve.wait_ge(chain, tap_at[c])
                            note(v.scalar_tensor_tensor(acc[:, c, :], upad[:, c, k:k + T], w, acc[:, c, :], ALU.mult,
                                                        ALU.add))
                        tap_at[c] = count[0]

                tap_at = [0] * 4
                conv(16)
                dve.wait_ge(main.done["cols"], C + 10)
                for t in range(TT):
                    note(v.tensor_copy(qk[:, t, NH:2 * NH, NOPE:QK],
                                       ptok[:, t, QL + KVL:TOKW].unsqueeze(1).to_broadcast([P, NH, ROPE])))
                    for h in range(2):
                        kv = bank[KV_BANKS[t][h]][:, :].rearrange("p (h d) -> p h d", h=4)
                        note(v.tensor_copy(qk[:, t, NH + 4 * h:NH + 4 * h + 4, 0:NOPE], kv[:, :, 0:NOPE]))
                        ins = v.tensor_copy(v2[:, t, 4 * h:4 * h + 4, :], kv[:, :, NOPE:])
                        if (t, h) == (1, 1):
                            ins.then_inc(ev("k_out"), 1)
                for m in range(10, 13):
                    lo_piece(main, B + m, 0)
                dve.wait_ge(ev("qk_sq"), l + 1)
                link(v.tensor_reduce(hsq[:, :], sq2[:].rearrange("p t h d -> p (t h) d"), AX, ALU.add))
                v.tensor_scalar(hvar[:, :], hsq[:, :], 1.0 / QK, EPS, ALU.mult, ALU.add).then_inc(ev("qk_var"), 1)
                dve.wait_ge(ev("qk_std"), l + 1)
                link(v.reciprocal(hrstd[:, :], hstd[:, :]))
                qkf = qk[:].rearrange("p t h d -> p (t h) d")
                link(v.tensor_tensor(qkf, qkf, hrstd[:, :].unsqueeze(2).to_broadcast([P, TT * 2 * NH, QK]), ALU.mult))
                for t in range(TT):
                    for g in range(2):
                        hs = qk[:, t, NH * g:NH * g + NH, :]
                        note(v.tensor_tensor(hs, hs, qkg[:, l, g, :].unsqueeze(1).to_broadcast([P, NH, QK]), ALU.mult))
                settle()
                half = ROPE // 2
                for t in range(TT):
                    xa, xb = qk[:, t, :, NOPE:NOPE + half], qk[:, t, :, NOPE + half:QK]
                    cos = ropet[:, t, 0:half].unsqueeze(1).to_broadcast([P, 2 * NH, half])
                    sin = ropet[:, t, half:ROPE].unsqueeze(1).to_broadcast([P, 2 * NH, half])
                    for n, (a, b) in enumerate(((xa, cos), (xb, sin), (xa, sin), (xb, cos))):
                        note(v.tensor_tensor(rt[:, n, t, :, :], a, b, ALU.mult))
                settle()
                for t in range(TT):
                    xa, xb = qk[:, t, :, NOPE:NOPE + half], qk[:, t, :, NOPE + half:QK]
                    v.tensor_tensor(xa, rt[:, 0, t, :, :], rt[:, 1, t, :, :], ALU.subtract)
                    ins = v.tensor_tensor(xb, rt[:, 2, t, :, :], rt[:, 3, t, :, :], ALU.add)
                ins.then_inc(ev("qk_ready"), 1)
                conv(16)
                for i in range(NH + 1):
                    if i < NH:
                        h = i
                        dve.wait_ge(ev("score_out"), 8 * l + h + 1)
                        b = bank[h % 2]
                        note(v.memset(b[0:64, 64:P], NEG))
                        note(v.memset(b[0:64, P + 192:P + T], NEG))
                        settle()
                        note(v.tensor_reduce(nmax[:, 2 * h:2 * h + 1], b[:, 0:P], AX, ALU.max))
                        note(v.tensor_reduce(nmax[:, 2 * h + 1:2 * h + 2], b[:, P:3 * P], AX, ALU.max))
                        settle()
                        v.tensor_scalar(negm[:, 2 * h:2 * h + 2], nmax[:, 2 * h:2 * h + 2], -SCALE, None,
                                        ALU.mult).then_inc(ev("neg_max"), 1)
                    if i >= 1:
                        h = i - 1
                        dve.wait_ge(ev("prob_turned"), 8 * l + h + 1)
                        if h >= 2:
                            dve.wait_ge(ev("att_out"), 8 * l + h - 1)
                        v.tensor_copy(probT[:, h % 2, :], bank[4 + h % 2][:, 0:3 * P]).then_inc(ev("probT_out"), 1)
                    conv(12)
                conv(len(taps))
                settle()
                mark(ev("conv31_out"))
                dve.wait_ge(ev("att_out"), 8 * (l + 1))
                link(v.reciprocal(rsum[:].rearrange("p t h -> p (t h)"), psum_p[:, :]))
                for t in range(TT):
                    ins = v.tensor_tensor(xn[:, t, 0:512].rearrange("p (h d) -> p h d", h=NH),
                                          bank[6 + t][:, :].rearrange("p (h d) -> p h d", h=NH),
                                          rsum[:, t, :].unsqueeze(2).to_broadcast([P, NH, VD]), ALU.mult)
                ins.then_inc(ev("att_ready"), 1)
                dve.wait_ge(ev("c_turned"), l + 1)
                for t in range(TT):
                    note(v.bn_stats(bns[:, t, 0, :], bank[2 + t][:, :]))
                settle()
                for t in range(TT):
                    note(v.bn_aggr(bna[:, t, :], bns[:, t, 0, :]))
                settle()
                v.tensor_scalar(var[:, 2:4], bna[:, :, 1], EPS, None, ALU.add).then_inc(ev("c_var"), 1)
                dve.wait_ge(ev("c_std"), l + 1)
                link(v.reciprocal(rstd[:, 2:4], std[:, 2:4]))
                for t in range(TT):
                    ins = v.tensor_scalar(xn[:, t, 512:1024], bank[2 + t][:, :], bna[:, t, 0:1], rstd[:, 2 + t:3 + t],
                                          ALU.subtract, ALU.mult)
                ins.then_inc(ev("c_ready"), 1)
                for b in range(2):
                    dve.wait_ge(ev("cath_out"), 3 * l + b + 1)
                    v.tensor_tensor(xl[:, 2 * b:2 * b + 2, :], bank[CAT_BANKS[b]][:, :].rearrange(
                        "p (c t) -> p c t", c=2), xh[:, 2 * b:2 * b + 2, :].bitcast(F32),
                        ALU.subtract).then_inc(ev("catl_out"), 1)
                dve.wait_ge(ev("cath_out"), 3 * (l + 1))
                v.tensor_tensor(xl[:, 4:8, :], acc[:, :, :], xh[:, 4:8, :].bitcast(F32),
                                ALU.subtract).then_inc(ev("catl_out"), 1)
                lo_piece(main, B + 13, 0)
                add_down(1.0, st["R"] + 4)

            v.memset(zeros[:].bitcast(F32), 0.0).then_inc(ev("const_vec"), 1)
            for S, inc in ((again.hi_done, RING), (again.lo_done, RING), (again.done["rows"], 1)):
                mark(S, inc)
            for s in range(RING):
                mark(again.raw_full[s], 16)
            mark(ev("spill_set"))
            dve.wait_ge(ev("const_pool"), N_POOL)
            for g, w in enumerate(WINDOWS):
                pr, c = slice(g % 2 * 64, g % 2 * 64 + 64), g // 2
                note(v.tensor_scalar(invc[pr, c, :], invc[pr, c, :], float(w), None, ALU.min))
            settle()
            note(v.reciprocal(invc[:], invc[:]))
            for tile in range(4):
                dve.wait_ge(ev("chan_turned"), tile + 1)
                v.tensor_copy(chan[:, tile, 0:used[tile]], bank[tile][:, 0:used[tile]]).then_inc(ev("chan_out"), 1)
            for l in range(2):
                dve.wait_ge(ev("ws_turned"), l + 1)
                note(v.tensor_copy(wsT[:, l, :, :], bank[4 + l][:, :].rearrange("p (h i) -> p h i", h=SH)))
            settle()
            v.memset(wsT[64:P, :, :, 0:64].rearrange("p l h i -> p (l h) i"), 0.0).then_inc(ev("const_vec"), 1)
            settle()
            dve.wait_ge(ev("chan_out"), 4)
            for st in stages:
                k = st["kind"]
                stats(st)
                if k == "post":
                    if st["layer"] == 2:
                        dve.wait_ge(ev("post1_in"), 16)
                    for t in range(TT):
                        ins = v.scalar_tensor_tensor(x[:, t, :], x[:, t, :], rstd[:, t:t + 1],
                                                     vecs[:, (1, 2, 0)[st["layer"]], :], ALU.mult, ALU.mult)
                    ins.then_inc(x_done, 1)
                    continue
                for t in range(TT):
                    v.tensor_scalar(xn[:, t, :], x[:, t, :], rstd[:, t:t + 1], None, ALU.mult).then_inc(xn_done, 1)
                for c in range(KD):
                    dve.wait_ge(xh_done, KD * st["M"] + bank_end(c, KD))
                    turned_rest(xl[:, c, :], bank[DOWN[c // 2]][:, c % 2 * T:(c % 2 + 1) * T], gain_of(st, c),
                                xh[:, c, :], xl_done)
                if k == "mix1":
                    mix1(st)
                elif k == "mix2":
                    mix2(st)
                elif k == "moe":
                    router(st)
                    experts(main, st, 0)
                    flag = dve.value_load(spill[0:1, 0:1])
                    with dve.If(flag > 0):
                        experts(again, SPILL, 1)
                        dve.nop()
                    dve.end_ifs()
                    mark(x_done)
                else:
                    ffn(main, st, T)
                    add_down(1.0 if k == "ffn1" else 0.5, st["R"] + st["n"])


N_SMALL = 11
N_POOL = 5
N_VEC = 2

NAMES = [
    "x", "norm1_g", "w_in", "pool_w", "pool_scale", "sgu_ln_g", "sgu_ln_b", "sgu_w", "sgu_b", "conv_w", "group_g",
    "w_out", "norm2_g", "ffn_w_gate", "ffn_w_up", "ffn_w_down", "router_w", "router_b", "moe_w_gate", "moe_w_up",
    "moe_w_down", "final_g", "ffn1_norm_2", "ffn1_w_gate_2", "ffn1_w_up_2", "ffn1_w_down_2", "mix_norm_2",
    "w_in_2", "q_latent_norm_2", "w_uq_2", "kv_latent_norm_2", "w_ukv_2", "q_norm_2", "k_norm_2", "conv_w_2",
    "conv_b_2", "conv_ln_g_2", "conv_ln_b_2", "w_out_2", "ffn2_norm_2", "ffn2_w_gate_2", "ffn2_w_up_2",
    "ffn2_w_down_2", "post_norm_2",
]


def kernel(**inputs):
    import concourse.bacc as bacc
    from concourse.bass_utils import run_bass_kernel_spmd as run

    nc = bacc.Bacc("TRN2", target_bir_lowering=False, num_devices=1)
    arrays, A = {}, {}
    for name in NAMES:
        a = np.ascontiguousarray(inputs[name])
        arrays[f"in_{name}"] = a
        A[name] = nc.dram_tensor(f"in_{name}", a.shape, mybir.dt.from_np(a.dtype), kind="ExternalInput").ap()
    arrays["rope_table"] = rope_tables()
    rope = nc.dram_tensor("rope_table", (T, ROPE), F32, kind="ExternalInput").ap()
    out = nc.dram_tensor("out", (1, T, D), F32, kind="ExternalOutput").ap()
    build(nc, A, rope, out)
    return run(nc, [arrays], core_ids=[0]).results[0]["out"]
```

```python
from contextlib import ExitStack

import numpy as np
import concourse.bass as bass
from concourse import mybir

F32 = mybir.dt.float32
F32R = mybir.dt.float32r
I32 = mybir.dt.int32
ACT = mybir.ActivationFunctionType
ALU = mybir.AluOpType
AX = mybir.AxisListType.X

P = 128
T = 256
TT = T // P
D = 1024
KD = D // P
F1 = 3584
F2 = 2816
FW = 256
NE = 8
PIECE = KD * FW
RING = 6
HRING = 3
EPS = 1e-6
DP, DS, DC = 256, 512, 256
WINDOWS = (2, 4, 8, 16)
PAD = 16
SH = 4
CW = 3
NH, QK, NOPE, ROPE, VD = 8, 96, 64, 32, 64
QL, KVL = 384, 256
CK = 31
CPAD = CK - 1
TOKW = QL + KVL + ROPE
NEG = -1e30
SCALE = float(QK) ** -0.5
THETA = 10000.0

STEPS1 = F1 // FW
STEPS2 = F2 // FW
MIX1_PIECES = 12
MIX2_PIECES = 14


def rope_tables():
    pos = np.arange(T, dtype=np.float32)
    inv = (1.0 / (THETA ** (np.arange(0, ROPE, 2, dtype=np.float32) / ROPE))).astype(np.float32)
    ang = (pos[:, None] * inv[None, :]).astype(np.float32)
    return np.concatenate([np.cos(ang), np.sin(ang)], axis=1).astype(np.float32)


def plan():
    stages = []
    at = dict(B=0, S=0, M=0, W=0)

    def stage(kind, layer, pieces, steps=0, **more):
        stages.append(dict(kind=kind, layer=layer, Q=len(stages), **at, **more))
        at["B"] += pieces
        at["S"] += steps
        at["M"] += kind != "post"
        at["W"] += kind not in ("post", "moe")

    for l in range(2):
        stage("mix1", l, MIX1_PIECES)
        if l == 0:
            stage("ffn1", 0, 3 * STEPS1, STEPS1, n=STEPS1)
        else:
            stage("moe", 0, 3 * STEPS1 * NE, STEPS1 * NE, n=STEPS1)
    stage("post", 0, 0)
    for l in range(2):
        stage("ffn2a", l, 3 * STEPS2, STEPS2, n=STEPS2)
        stage("mix2", l, MIX2_PIECES)
        stage("ffn2b", l, 3 * STEPS2, STEPS2, n=STEPS2)
        stage("post", 1 + l, 0)
    return stages


def build(nc, A, rope, out):
    stages = plan()

    with ExitStack() as ctx:
        def sb(name, shape, dt=F32):
            return ctx.enter_context(nc.sbuf_tensor(name, shape, dt))

        def sem(name):
            return ctx.enter_context(nc.semaphore(name))

        raw = sb("raw", [P, RING, PIECE])
        lo = nc.alloc_sbuf_tensor_at("lo", [P, RING, PIECE], F32R, offset=nc.sbuf_base - 4 * RING * PIECE)
        hi = sb("hi", [P, HRING, PIECE], F32R)
        x = sb("x", [P, TT, D])
        xn = sb("xn", [P, TT, D])
        xh = sb("xh", [P, KD, T], F32R)
        xl = sb("xl", [P, KD, T], F32R)
        sg = sb("sg", [P, 2, T])
        hf = sb("hf", [P, 2, T])
        hh = sb("hh", [P, 2, T], F32R)
        hl = sb("hl", [P, 2, T], F32R)
        ident = sb("ident", [P, P])
        ones = sb("ones", [P, P])
        before = sb("before", [P, P])
        slots = sb("slots", [P, P])
        zeros = sb("zeros", [P, 512], F32R)
        earlier = sb("earlier", [P, NE, NE])
        invc = sb("invc", [P, 2, T])
        chan = sb("chan", [P, 3, P])
        ropet = sb("ropet", [P, TT, ROPE])
        gains = sb("gains", [P, 2, D])
        lng = sb("lng", [P, DS])
        lnb = sb("lnb", [P, DS])
        psc = sb("psc", [P, DP])
        poolw = sb("poolw", [P, 2, 2, P])
        wsT = sb("wsT", [P, 2, SH, P])
        qkg = sb("qkg", [P, 2, 2, QK])
        routw = sb("routw", [P, KD, NE])
        rwh = sb("rwh", [P, KD, NE], F32R)
        rwl = sb("rwl", [P, KD, NE], F32R)
        routb = sb("routb", [P, NE])
        ssq = sb("ssq", [P, 8])
        var = sb("var", [P, 8])
        std = sb("std", [P, 8])
        rstd = sb("rstd", [P, 8])
        bns = sb("bns", [P, TT, 2, 6])
        bna = sb("bna", [P, TT, 2])
        hsq = sb("hsq", [P, TT * 2 * NH])
        hvar = sb("hvar", [P, TT * 2 * NH])
        hstd = sb("hstd", [P, TT * 2 * NH])
        hrstd = sb("hrstd", [P, TT * 2 * NH])
        nmax = sb("nmax", [P, TT * NH])
        psum_p = sb("psum_p", [P, TT * NH])
        rsum = sb("rsum", [P, TT, NH])
        negm = sb("negm", [P, TT * NH])
        logit = sb("logit", [P, TT, NE])
        big = sb("big", [P, TT, NE * NE])
        big2 = sb("big2", [P, TT, NE * NE])
        place = sb("place", [P, TT, NE])
        sel = sb("sel", [P, TT, NE])
        top = sb("top", [P, TT])
        ex = sb("ex", [P, TT, NE])
        den = sb("den", [P, TT])
        rden = sb("rden", [P, TT])
        gates = sb("gates", [P, TT, NE])
        rank = sb("rank", [P, TT, 2, NE + 1])
        most = sb("most", [P, 1])
        spill = sb("spill", [1, 1], I32)
        touch = sb("touch", [P, 32])

        ARENA = 53 * 1024
        arena = sb("arena", [P, ARENA // 4])
        base = nc.sbuf_base - ARENA

        class Scratch:
            def __init__(self):
                self.at = 0

            def __call__(self, name, shape, dt=F32):
                t = nc.alloc_sbuf_tensor_at(name, shape, dt, offset=base + self.at)
                self.at += 4 * int(np.prod(shape[1:]))
                self.at += -self.at % 32
                assert self.at <= ARENA, (name, self.at)
                return t

        s0 = Scratch()
        stage_rows = s0("stage_rows", [P, 3, P])
        stage_ws = s0("stage_ws", [P, 2, SH, P])
        s1 = Scratch()
        apad = s1("apad", [P, 2, PAD + T])
        w2 = s1("w2", [P, 2, PAD + T])
        w4 = s1("w4", [P, 2, PAD + T])
        w8 = s1("w8", [P, 2, PAD + T])
        w16 = s1("w16", [P, 2, PAD + T])
        dT = s1("dT", [P, 2, T])
        gcT = s1("gcT", [P, 2, T])
        zpad = s1("zpad", [P, 2, CW - 1 + T])
        zc = s1("zc", [P, 2, T])
        gb = s1("gb", [P, TT, DC])
        u1 = s1("u1", [P, TT, DS])
        vn = s1("vn", [P, TT, DS])
        y1 = s1("y1", [P, TT, D])
        s2 = Scratch()
        h2h = s2("h2h", [P, TT, D], F32R)
        h2l = s2("h2l", [P, TT, D], F32R)
        yh = s2("yh", [P, D], F32R)
        yl = s2("yl", [P, D], F32R)
        pick = s2("pick", [P, TT, P], F32R)
        pickT = s2("pickT", [P, T], F32R)
        s3 = Scratch()
        ptok = s3("ptok", [P, TT, TOKW])
        qk = s3("qk", [P, TT, 2 * NH, QK])
        v2 = s3("v2", [P, TT, NH, VD])
        upad = s3("upad", [P, 4, CPAD + T])
        acc = s3("acc", [P, 4, T])
        prob = s3("prob", [P, 2, 3 * P])
        probT = s3("probT", [P, 2, 3 * P])
        at_qkT = s3.at
        qkT = s3("qkT", [P, 2 * NH, T])
        s3.at = at_qkT
        sq2 = s3("sq2", [P, TT, 2 * NH, QK])
        s3.at = at_qkT
        rt = s3("rt", [P, 4, TT, 2 * NH, ROPE // 2])

        bank = [ctx.enter_context(nc.psum_tensor(f"bank{i}", [P, 512], F32)) for i in range(8)]
        DOWN = (2, 3, 4, 5)
        GATE, UP, TURNED_H = 0, 1, 7

        class Ring:

            def __init__(self, tag):
                self.raw_full = [sem(f"{tag}raw_full{s}") for s in range(RING)]
                self.hi_done = sem(f"{tag}hi_done")
                self.lo_done = sem(f"{tag}lo_done")
                self.multiplied = sem(f"{tag}multiplied")
                self.sg_done = sem(f"{tag}sg_done")
                self.hf_done = sem(f"{tag}hf_done")
                self.hh_done = sem(f"{tag}hh_done")
                self.hl_done = sem(f"{tag}hl_done")
                self.ht_done = sem(f"{tag}ht_done")
                self.pick_done = sem(f"{tag}pick_done")
                self.gathered = sem(f"{tag}gathered")
                self.gh_done = sem(f"{tag}gh_done")
                self.gl_done = sem(f"{tag}gl_done")
                self.pick_turned = sem(f"{tag}pick_turned")
                self.pickT_done = sem(f"{tag}pickT_done")
                self.yh_done = sem(f"{tag}yh_done")
                self.yl_done = sem(f"{tag}yl_done")
                self.spread = sem(f"{tag}spread")
                self.added = sem(f"{tag}added")

        main = Ring("")
        again = Ring("spill_")
        x_loaded = [sem(f"x_loaded{t}") for t in range(TT)]
        gain_in = [sem(f"gain_in{i}") for i in range(2)]
        first_tile = sem("first_tile")
        x_done = sem("x_done")
        ssq_done = sem("ssq_done")
        var_done = sem("var_done")
        std_done = sem("std_done")
        xn_done = sem("xn_done")
        turned = sem("turned")
        xh_done = sem("xh_done")
        xl_done = sem("xl_done")
        chain = sem("chain")
        achain = sem("achain")
        pchain = sem("pchain")
        stored = sem("stored")
        E = {}

        def ev(name):
            if name not in E:
                E[name] = sem(name)
            return E[name]

        staged, where, used = [], {}, [0, 0, 0]

        def put(tile, name, ap, n):
            staged.append((tile, used[tile], n, ap.rearrange("(r c) -> r c", c=P)))
            where[name] = (tile, used[tile])
            used[tile] += n

        for l in range(2):
            put(0, ("group", l), A["group_g"][l], KD)
            put(0, ("cw", l), A["conv_w"][l].rearrange("a c -> (a c)"), CW * 2)
            put(0, ("cb", l), A["conv_b_2"][l], 4)
            put(0, ("clg", l), A["conv_ln_g_2"][l], 4)
            put(0, ("clb", l), A["conv_ln_b_2"][l], 4)
            put(0, ("ql", l), A["q_latent_norm_2"][l], QL // P)
            put(0, ("kvl", l), A["kv_latent_norm_2"][l], KVL // P)
            put(0, ("sb", l), A["sgu_b"][l].rearrange("h i -> (h i)"), SH)
            put(1 + l, ("cw2", l), A["conv_w_2"][l].rearrange("a c -> (a c)"), CK * 4)

        def col(name, i):
            tile, at = where[name]
            return chan[:, tile, at + i:at + i + 1]

        def gain_of(st):
            l = st["layer"]
            if st["kind"] == "post":
                return A["final_g"] if l == 0 else A["post_norm_2"][l - 1]
            if st["kind"] == "moe":
                return A["norm2_g"][1]
            return A[{"mix1": "norm1_g", "ffn1": "norm2_g", "ffn2a": "ffn1_norm_2", "mix2": "mix_norm_2",
                      "ffn2b": "ffn2_norm_2"}[st["kind"]]][l]

        def after(st):
            return next((n for n in stages[st["Q"] + 1:] if n["kind"] != "post"), None)

        def cols_view(w):
            return w.rearrange("(k p) f -> p k f", p=P)

        def rows_view(w):
            return w.rearrange("(s p) d -> p s d", p=P)

        def weights_of(st):
            l = st["layer"]
            if st["kind"] == "ffn1":
                return A["ffn_w_gate"][0], A["ffn_w_up"][0], A["ffn_w_down"][0]
            w = "ffn1" if st["kind"] == "ffn2a" else "ffn2"
            return A[f"{w}_w_gate_2"][l], A[f"{w}_w_up_2"][l], A[f"{w}_w_down_2"][l]

        MIX1_COLS = (768, 1024, 0, 1536, 1792, 1280, 256, 512)
        MIX1_BANKS = (0, 1, 6, 7, 2, 3, 4, 5)
        MIX2_COLS = ((0, 256), (256, 256), (512, 160), (672, 256), (928, 256), (1184, 256), (1440, 256))
        MIX2_BANKS = (0, 1, 6, 7, 2, 3, 4)
        Q_BANKS = ((6, 7), (2, 3))
        KV_BANKS = ((4, 5), (0, 1))
        TURN4 = (6, 7, 2, 3)
        Y_BANKS = (0, 1, 6, 7)
        CAT_BANKS = (0, 1, 4, 5)

        def bank_end(c, n):
            return min(n, c // 2 * 2 + 2)

        def whole(b):
            return b[:, :].rearrange("p (s t) -> p s t", s=2)

        def turned_h():
            return bank[TURNED_H][:, 0:2 * P].rearrange("p (s t) -> p s t", s=2)

        SPILL = dict(kind="moe", layer=0, n=STEPS1, B=RING, S=1)

        def sp_load(sp, S, c, i, src, shape):
            n = shape[0] * shape[1]
            if not isinstance(i, int) or c >= RING:
                sp.wait_ge(S.multiplied, c - RING + 1 + 6 * i)
            dst = raw[:, c % RING, 0:n].rearrange("p (a b) -> p a b", a=shape[0])
            sp.dma_start(dst, src).then_inc(S.raw_full[c % RING], 16)

        def gate_at(B, m):
            return B - 1 + 3 * m if m else B

        def rows_at(B, m):
            return B + 4 + 3 * m if m >= 0 else B - 1

        def in_steps(eng, n, step):
            step(1, 1, 0)
            with eng.Fori(0, (n - 2) // 2) as q:
                step(2 + 2 * q, 2, q)
                step(3 + 2 * q, 3, q)
            if n % 2:
                step(n - 1, n - 1, 0)

        def sp_ffn(sp, S, st, wg, wu, wd, e=0):
            B, n = st["B"], st["n"]
            i0 = n // 2 * e

            def gu(w, j):
                return w[:, :, bass.ds(j * FW, FW)]

            sp_load(sp, S, B, i0, wg[:, :, 0:FW], (KD, FW))
            sp_load(sp, S, B + 1, i0, wu[:, :, 0:FW], (KD, FW))

            def step(j, m, q):
                sp_load(sp, S, gate_at(B, m), i0 + q, gu(wg, j), (KD, FW))
                sp_load(sp, S, gate_at(B, m) + 1, i0 + q, gu(wu, j), (KD, FW))
                sp_load(sp, S, rows_at(B, m - 1), i0 + q, wd[:, bass.ds((j - 1) * 2, 2), :], (2, D))

            in_steps(sp, n, step)
            sp_load(sp, S, B + 3 * n - 1, i0, wd[:, 2 * (n - 1):2 * n, :], (2, D))

        def sp_experts(sp, S, st):
            wg = A["moe_w_gate"][0].rearrange("e (k p) f -> e p k f", p=P)
            wu = A["moe_w_up"][0].rearrange("e (k p) f -> e p k f", p=P)
            wd = A["moe_w_down"][0].rearrange("e (s p) d -> e p s d", p=P)
            with sp.Fori(0, NE) as e:
                sp_ffn(sp, S, st, wg[e], wu[e], wd[e], e)

        block = ctx.enter_context(nc.Block())

        @block.sync
        def _(sp):
            for st in stages:
                k, l = st["kind"], st["layer"]
                if k == "mix1":
                    w = cols_view(A["w_in"][l])
                    for m, c0 in enumerate(MIX1_COLS):
                        sp_load(sp, main, st["B"] + m, 0, w[:, :, c0:c0 + FW], (KD, FW))
                    w = rows_view(A["w_out"][l])
                    for m in range(4):
                        sp_load(sp, main, st["B"] + 8 + m, 0, w[:, 2 * m:2 * m + 2, :], (2, D))
                elif k == "mix2":
                    w = cols_view(A["w_in_2"][l])
                    for m, (c0, cn) in enumerate(MIX2_COLS):
                        sp_load(sp, main, st["B"] + m, 0, w[:, :, c0:c0 + cn], (KD, cn))
                    w = rows_view(A["w_uq_2"][l])
                    sp_load(sp, main, st["B"] + 7, 0, w[:, 0:2, :], (2, NH * QK))
                    sp_load(sp, main, st["B"] + 8, 0, w[:, 2:3, :], (1, NH * QK))
                    sp_load(sp, main, st["B"] + 9, 0, rows_view(A["w_ukv_2"][l]), (2, D))
                    w = rows_view(A["w_out_2"][l])
                    for m in range(4):
                        sp_load(sp, main, st["B"] + 10 + m, 0, w[:, 2 * m:2 * m + 2, :], (2, D))
                elif k == "moe":
                    sp_experts(sp, main, st)
                    sp.wait_ge(ev("spill_known"), 1)
                    flag = sp.value_load(spill[0:1, 0:1])
                    with sp.If(flag > 0):
                        sp.wait_ge(main.added, 4 * NE + 1)
                        sp.wait_ge(ev("spill_set"), 1)
                        sp_experts(sp, again, SPILL)
                        sp.wait_ge(again.added, 4 * NE + 1)
                        sp.nop()
                    sp.end_ifs()
                elif k in ("ffn1", "ffn2a", "ffn2b"):
                    wg, wu, wd = weights_of(st)
                    sp_ffn(sp, main, st, cols_view(wg), cols_view(wu), rows_view(wd))
            for t in range(TT):
                sp.wait_ge(x_done, TT * (len(stages) - 1) + t + 1)
                sp.dma_start(out[0, t * P:t * P + P, :], x[:, t, :]).then_inc(stored, 16)
            sp.wait_ge(stored, 16 * TT)

        def act_hi(act, S, c, i, n=PIECE):
            act.wait_ge(S.raw_full[c % RING], 16 * (c // RING + 1 + i))
            if not isinstance(i, int) or c >= HRING:
                act.wait_ge(S.multiplied, c - HRING + 1 + 6 * i)
            nc.scalar.copy(hi[:, c % HRING, 0:n], raw[:, c % RING, 0:n]).then_inc(S.hi_done, 1)

        def act_silu(act, S, c, i, t, by_token):
            act.wait_ge(S.multiplied, c + 1 + 6 * i)
            act.wait_ge(S.hf_done, t)
            o, i = (sg[:, 0, :], bank[GATE][:, 0:FW]) if by_token else (sg[:, :, :], whole(bank[GATE]))
            nc.scalar.activation(o, i, ACT.Silu).then_inc(S.sg_done, 1)

        def act_round_h(act, S, c, i, t, by_token, turned0=0):
            act.wait_ge(S.multiplied, c + 1 + 6 * i)
            if by_token:
                act.wait_ge(S.ht_done, t + 1 - turned0)
                nc.scalar.copy(hh[:, :, 0:P], turned_h()).then_inc(S.hh_done, 1)
            else:
                act.wait_ge(S.hf_done, t + 1)
                nc.scalar.copy(hh[:, :, :], hf[:, :, :]).then_inc(S.hh_done, 1)

        def act_step(act, S, st, e, by_token):
            B, S0, i0 = st["B"], st["S"] + st["n"] * e, st["n"] // 2 * e

            def step(j, m, q):
                act_silu(act, S, gate_at(B, m - 1), i0 + q, S0 + j - 1, by_token)
                act_hi(act, S, gate_at(B, m), i0 + q)
                act_hi(act, S, gate_at(B, m) + 1, i0 + q)
                act_hi(act, S, rows_at(B, m - 1), i0 + q)
                act_round_h(act, S, rows_at(B, m - 2), i0 + q, S0 + j - 1, by_token, st["S"])
            return step

        def act_ffn(act, st):
            B, n, S0 = st["B"], st["n"], st["S"]
            in_steps(act, n, act_step(act, main, st, 0, False))
            act_silu(act, main, gate_at(B, n - 1), 0, S0 + n - 1, False)
            act_hi(act, main, B + 3 * n - 1, 0)
            act_round_h(act, main, rows_at(B, n - 2), 0, S0 + n - 1, False)

        def act_ahead(act, st):
            act_hi(act, main, st["B"], 0)
            act_hi(act, main, st["B"] + 1, 0)

        def act_stats(act, st):
            q = st["Q"]
            nc.scalar.preload_act_table(ACT.Sqrt)
            for t in range(TT):
                if q == 0:
                    act.wait_ge(x_loaded[t], 16)
                else:
                    act.wait_ge(x_done, TT * (q - 1) + t + 1)
                nc.scalar.activation(xn[:, t, :], x[:, t, :], ACT.Square,
                                     accum_out=ssq[:, t:t + 1]).then_inc(ssq_done, 1)
            for t in range(TT):
                act.wait_ge(var_done, TT * q + t + 1)
                nc.scalar.activation(std[:, t:t + 1], var[:, t:t + 1], ACT.Sqrt).then_inc(std_done, 1)

        def norm_bank(b):
            return bank[DOWN[b]][:, :].rearrange("p (k t) -> p k t", k=4)

        def norm_part(a, b):
            return a[:, b % 2 * 4:b % 2 * 4 + 4, b // 2 * P:b // 2 * P + P]

        def act_turned(act, st):
            for b in range(4):
                act.wait_ge(turned, 4 * st["M"] + b + 1)
                nc.scalar.copy(norm_part(xh, b), norm_bank(b)).then_inc(xh_done, 1)

        def act_gathered(act, S, e):
            for b in range(2):
                act.wait_ge(S.gathered, 4 * e + b + 1)
                nc.scalar.copy(xh[:, 4 * b:4 * b + 4, 0:P],
                               bank[4 + b][:, :].rearrange("p (k s) -> p k s", k=4)).then_inc(S.gh_done, 1)

        def act_experts(act, S, st):
            B, n = st["B"], st["n"]
            nc.scalar.preload_act_table(ACT.Silu)
            act_gathered(act, S, 0)
            if S is again:
                act_hi(act, S, B, 0)
                act_hi(act, S, B + 1, 0)
            act_step(act, S, st, 0, True)(1, 1, 0)

            def expert(e, last):
                S0, i0 = st["S"] + n * e, n // 2 * e
                step = act_step(act, S, st, e, True)
                with act.Fori(0, n // 2 - 2) as q:
                    step(2 + 2 * q, 2, q)
                    step(3 + 2 * q, 3, q)
                step(n - 2, n - 2, 0)
                act.wait_ge(S.pick_turned, e + 1)
                nc.scalar.copy(pickT[:, :], bank[5][:, 0:T]).then_inc(S.pickT_done, 1)
                step(n - 1, n - 1, 0)
                act_silu(act, S, gate_at(B, n - 1), i0, S0 + n - 1, True)
                act_hi(act, S, B + 3 * n - 1, i0)
                if not last:
                    act_hi(act, S, B + 3 * n, i0)
                    act_gathered(act, S, e + 1)
                act_round_h(act, S, rows_at(B, n - 2), i0, S0 + n - 1, True, st["S"])
                if not last:
                    act_hi(act, S, B + 3 * n + 1, i0)
                act.wait_ge(S.multiplied, B + 3 * n + 6 * i0)
                for b in range(2):
                    nc.scalar.copy(yh[:, 512 * b:512 * b + 512], bank[2 + b][:, :]).then_inc(S.yh_done, 1)
                if not last:
                    act_step(act, S, st, e + 1, True)(1, 1, 0)

            with act.Fori(0, NE - 1) as e:
                expert(e, False)
            expert(NE - 1, True)

        def act_mix1(act, st):
            B, l = st["B"], st["layer"]
            for m in range(2, 6):
                act_hi(act, main, B + m, 0)
            act.wait_ge(main.multiplied, B + 3)
            act.wait_ge(ev("pads"), l + 1)
            nc.scalar.copy(apad[:, :, PAD:], bank[6][:, :].rearrange("p (c t) -> p c t", c=2)).then_inc(ev("a_out"), 1)
            act_hi(act, main, B + 6, 0)
            act.wait_ge(main.multiplied, B + 4)
            nc.scalar.copy(gcT[:, :, :], bank[7][:, :].rearrange("p (c t) -> p c t", c=2)).then_inc(ev("gc_out"), 1)
            act.wait_ge(ev("v_var"), l + 1)
            nc.scalar.activation(std[:, 2:4], var[:, 2:4], ACT.Sqrt).then_inc(ev("v_std"), 1)
            act_hi(act, main, B + 7, 0)
            act_hi(act, main, B + 8, 0)
            act.wait_ge(main.multiplied, B + 6)
            nc.scalar.copy(gb[:, :, :], bank[3][:, :].rearrange("p (t c) -> p t c", t=2)).then_inc(ev("gb_out"), 1)
            for i in range(2):
                act_hi(act, main, B + 9 + i, 0)
                act.wait_ge(main.multiplied, B + 7 + i)
                nc.scalar.copy(u1[:, :, i * 256:i * 256 + 256],
                               bank[4 + i][:, :].rearrange("p (t c) -> p t c", t=2)).then_inc(ev("u_out"), 1)
            act.wait_ge(ev("y_raw"), l + 1)
            for t in range(TT):
                for g, (c0, c1) in enumerate(((0, DP), (DP, DP + DS), (DP + DS, D))):
                    nc.scalar.activation(xn[:, t, c0:c1], y1[:, t, c0:c1], ACT.Square,
                                         accum_out=ssq[:, 2 + 3 * t + g:3 + 3 * t + g]).then_inc(ev("y_sq"), 1)
            act.wait_ge(ev("y_var"), l + 1)
            nc.scalar.activation(std[:, 2:8], var[:, 2:8], ACT.Sqrt).then_inc(ev("y_std"), 1)
            nc.scalar.preload_act_table(ACT.Silu)
            for k in range(KD):
                act.wait_ge(ev("y_turned"), 4 * l + k // 2 + 1)
                nc.scalar.activation(xh[:, k, :], bank[Y_BANKS[k // 2]][:, k % 2 * T:(k % 2 + 1) * T], ACT.Copy,
                                     scale=col(("group", l), k)).then_inc(ev("yh_out"), 1)
            act_hi(act, main, B + 11, 0)

        def act_mix2(act, st):
            B, l = st["B"], st["layer"]
            for m in range(2, 4):
                act_hi(act, main, B + m, 0, KD * MIX2_COLS[m][1])
            for m in range(3):
                c0, cn = MIX2_COLS[m]
                act.wait_ge(main.multiplied, B + m + 1)
                nc.scalar.copy(ptok[:, :, c0:c0 + cn], bank[MIX2_BANKS[m]][:, :].rearrange(
                    "p (t c) -> p t c", t=2)[:, :, 0:cn]).then_inc(ev("ptok_out"), 1)
                act_hi(act, main, B + 4 + m, 0)
            for t in range(TT):
                for g, (c0, c1) in enumerate(((0, QL), (QL, QL + KVL))):
                    act.wait_ge(ev("ptok_out"), 3 * (l + 1))
                    nc.scalar.activation(xn[:, t, c0:c1], ptok[:, t, c0:c1], ACT.Square,
                                         accum_out=ssq[:, 2 + 2 * t + g:3 + 2 * t + g]).then_inc(ev("lat_sq"), 1)
            act.wait_ge(ev("lat_var"), l + 1)
            nc.scalar.activation(std[:, 2:6], var[:, 2:6], ACT.Sqrt).then_inc(ev("lat_std"), 1)
            act_hi(act, main, B + 7, 0, 2 * NH * QK)
            for i in range(2):
                act.wait_ge(main.multiplied, B + 6 + i)
                nc.scalar.activation(acc[:, 2 * i:2 * i + 2, :], bank[3 + i][:, :].rearrange("p (c t) -> p c t", c=2),
                                     ACT.Sigmoid).then_inc(ev("sig_out"), 1)
            act_hi(act, main, B + 8, 0, NH * QK)
            act_hi(act, main, B + 9, 0)
            for c in range(5):
                act.wait_ge(ev("lat_turned"), 3 * l + c // 2 + 1)
                g = col(("ql", l), c) if c < 3 else col(("kvl", l), c - 3)
                nc.scalar.activation(xh[:, c, :], bank[(5, 0, 1)[c // 2]][:, c % 2 * T:(c % 2 + 1) * T], ACT.Copy,
                                     scale=g).then_inc(ev("lath_out"), 1)
            act.wait_ge(main.multiplied, B + 9)
            for t in range(TT):
                for h in range(2):
                    nc.scalar.copy(qk[:, t, 4 * h:4 * h + 4, :], bank[Q_BANKS[t][h]][:, 0:4 * QK].rearrange(
                        "p (h d) -> p h d", h=4)).then_inc(ev("q_out"), 1)
            act_hi(act, main, B + 10, 0)
            act_hi(act, main, B + 11, 0)
            act_hi(act, main, B + 12, 0)
            act.wait_ge(ev("q_out"), 4 * (l + 1))
            act.wait_ge(ev("k_out"), l + 1)
            nc.scalar.activation(sq2[:], qk[:], ACT.Square).then_inc(ev("qk_sq"), 1)
            act.wait_ge(ev("qk_var"), l + 1)
            nc.scalar.activation(hstd[:, :], hvar[:, :], ACT.Sqrt).then_inc(ev("qk_std"), 1)
            nc.scalar.preload_act_table(ACT.Exp)
            for g in range(8):
                act.wait_ge(ev("qk_turned"), 8 * l + g + 1)
                nc.scalar.copy(qkT[0:QK, 2 * g:2 * g + 2, :], bank[TURN4[g % 4]][0:QK, :].rearrange(
                    "p (h t) -> p h t", h=2)).then_inc(ev("qkT_out"), 1)
            for h in range(NH):
                act.wait_ge(ev("neg_max"), 8 * l + h + 1)
                if h >= 2:
                    act.wait_ge(ev("prob_turned"), 8 * l + h - 1)
                for t in range(TT):
                    c0, c1 = (0, P) if t == 0 else (P, 3 * P)
                    nc.scalar.activation(prob[:, h % 2, c0:c1], bank[h % 2][:, c0:c1], ACT.Exp,
                                         bias=negm[:, 2 * h + t:2 * h + t + 1], scale=SCALE,
                                         accum_out=psum_p[:, t * NH + h:t * NH + h + 1]).then_inc(ev("exp_out"), 1)
            act.wait_ge(ev("c_var"), l + 1)
            nc.scalar.activation(std[:, 2:4], var[:, 2:4], ACT.Sqrt).then_inc(ev("c_std"), 1)
            nc.scalar.preload_act_table(ACT.Silu)
            for b in range(2):
                act.wait_ge(ev("cat_turned"), 4 * l + b + 1)
                nc.scalar.copy(xh[:, 2 * b:2 * b + 2, :], bank[CAT_BANKS[b]][:, :].rearrange(
                    "p (c t) -> p c t", c=2)).then_inc(ev("cath_out"), 1)
            for c in range(4):
                act.wait_ge(ev("cat_turned"), 4 * l + 3 + c // 2)
                nc.scalar.activation(acc[:, c, :], bank[CAT_BANKS[2 + c // 2]][:, c % 2 * T:(c % 2 + 1) * T],
                                     ACT.Silu, scale=col(("clg", l), c), bias=col(("clb", l), c)).then_inc(achain, 1)
            act.wait_ge(achain, 4 * (l + 1))
            nc.scalar.copy(xh[:, 4:8, :], acc[:, :, :]).then_inc(ev("cath_out"), 1)
            act_hi(act, main, B + 13, 0)

        @block.scalar
        def _(act):
            for t in range(TT):
                act.dma_start(x[:, t, :], A["x"][0, t * P:t * P + P, :]).then_inc(x_loaded[t], 16)
            for tile, at, n, ap in staged[::2]:
                act.dma_start(stage_rows[at:at + n, tile, :], ap).then_inc(ev("rows_in"), 16)
            act_ahead(act, stages[0])
            for st in stages:
                k = st["kind"]
                act_stats(act, st)
                if k == "post":
                    continue
                if k in ("ffn1", "ffn2a", "ffn2b"):
                    nc.scalar.preload_act_table(ACT.Silu)
                act_turned(act, st)
                if st["M"] == 0:
                    act.wait_ge(ev("chan_out"), 3)
                if k == "mix1":
                    act_mix1(act, st)
                elif k == "mix2":
                    act_mix2(act, st)
                elif k == "moe":
                    act.wait_ge(ev("small_in"), 16 * N_SMALL)
                    nc.scalar.copy(rwh[:], routw[:]).then_inc(ev("rwh_out"), 1)
                    act.wait_ge(xn_done, 4 * (st["M"] + 1))
                    for t in range(TT):
                        nc.scalar.copy(h2h[:, t, :], xn[:, t, :]).then_inc(ev("h2h_out"), 1)
                    act.wait_ge(ev("shifted"), 1)
                    nc.scalar.activation(ex[:], ex[:], ACT.Exp).then_inc(ev("ex_out"), 1)
                    act_experts(act, main, st)
                    act.wait_ge(ev("spill_known"), 1)
                    flag = act.value_load(spill[0:1, 0:1])
                    with act.If(flag > 0):
                        act.wait_ge(main.added, 4 * NE + 1)
                        act.wait_ge(ev("spill_set"), 1)
                        act_experts(act, again, SPILL)
                        act.wait_ge(again.added, 4 * NE + 1)
                        act.nop()
                    act.end_ifs()
                else:
                    act_ffn(act, st)
                if after(st):
                    act_ahead(act, after(st))

        def pe_cols(pe, S, c, i, bk, w, free=()):
            pe.wait_ge(S.lo_done, c + 1 + 6 * i)
            for s, v in free:
                pe.wait_ge(s, v)
            r, hr = c % RING, c % HRING
            for s in range(2):
                o = bank[bk][:, s * w:(s + 1) * w]
                for k in range(KD):
                    a = k * FW + s * P
                    pe.matmul(o, hi[:, hr, a:a + P], xh[:, k, 0:w], start=(k == 0), stop=False)
                    pe.matmul(o, hi[:, hr, a:a + P], xl[:, k, 0:w], start=False, stop=False)
                    mm = pe.matmul(o, lo[:, r, a:a + P], xh[:, k, 0:w], start=False, stop=(k == KD - 1))
            return mm

        def pe_toks(pe, c, bk, cn, ks=range(KD), x0=0, out0=0, stride=256, first=True, last=True, c0=0, row=None,
                    nt=TT):
            r, hr, row = c % RING, c % HRING, row or cn
            for t in range(nt):
                o = bank[bk[t]][:, t * stride:t * stride + cn]
                for n, k in enumerate(ks):
                    wgt = slice(n * row + c0, n * row + c0 + cn)
                    tk = slice(t * P, t * P + P)
                    pe.matmul(o, xh[:, x0 + k, tk], hi[:, hr, wgt], start=(first and n == 0), stop=False)
                    pe.matmul(o, xh[:, x0 + k, tk], lo[:, r, wgt], start=False, stop=False)
                    mm = pe.matmul(o, xl[:, x0 + k, tk], hi[:, hr, wgt], start=False, stop=(last and n == len(ks) - 1))
            return mm

        def pe_last_rows(pe, c, ah, al, first=False):
            pe.wait_ge(main.lo_done, c + 1)
            r, hr = c % RING, c % HRING
            for t in range(TT):
                tk = slice(t * P, t * P + P)
                for s in range(2):
                    for a, w in ((ah, hi[:, hr]), (ah, lo[:, r]), (al, hi[:, hr])):
                        for h in range(2):
                            wgt = slice(s * D + h * 512, s * D + h * 512 + 512)
                            mm = pe.matmul(bank[DOWN[2 * t + h]][:, :], a[:, s, tk], w[:, wgt], start=False,
                                           stop=(s == 1 and a is al), skip_group_check=True)
                mm.then_inc(first_tile if t == 0 else main.multiplied, 1)

        def pe_rows(pe, S, c, i, ah, al, nt, first=False, last=False):
            pe.wait_ge(S.lo_done, c + 1 + 6 * i)
            r, hr = c % RING, c % HRING
            for s in range(2):
                for t in range(nt):
                    tk = slice(t * P, t * P + P)
                    for h in range(2):
                        o = bank[DOWN[2 * t + h]][:, :]
                        wgt = slice(s * D + h * 512, s * D + h * 512 + 512)
                        pe.matmul(o, ah[:, s, tk], hi[:, hr, wgt], start=(first and s == 0), stop=False,
                                  skip_group_check=True)
                        pe.matmul(o, ah[:, s, tk], lo[:, r, wgt], start=False, stop=False, skip_group_check=True)
                    for h in range(2):
                        o = bank[DOWN[2 * t + h]][:, :]
                        wgt = slice(s * D + h * 512, s * D + h * 512 + 512)
                        mm = pe.matmul(o, al[:, s, tk], hi[:, hr, wgt], start=False, stop=(last and s == 1),
                                       skip_group_check=True)
            return mm.then_inc(S.multiplied, 1)

        def open_down(pe, nb):
            for b in range(nb):
                pe.matmul(bank[DOWN[b]][:, :], zeros[:, 0:P], zeros[:, :], start=True, stop=False,
                          skip_group_check=True)

        def pe_gate(pe, S, c, i, t, by_token):
            free = [(S.sg_done, t)]
            if by_token:
                pe_by_token(pe, S, c, i, GATE, free).then_inc(S.multiplied, 1)
            else:
                pe_cols(pe, S, c, i, GATE, T, free).then_inc(S.multiplied, 1)

        def pe_up(pe, S, c, i, t, by_token):
            free = [(S.hf_done, t)]
            if by_token:
                pe_by_token(pe, S, c, i, UP, free).then_inc(S.multiplied, 1)
            else:
                pe_cols(pe, S, c, i, UP, T, free).then_inc(S.multiplied, 1)

        def pe_by_token(pe, S, c, i, bk, free):
            pe.wait_ge(S.lo_done, c + 1 + 6 * i)
            for s, v in free:
                pe.wait_ge(s, v)
            return pe_toks(pe, c, (bk,), FW, nt=1)

        def pe_turn_h(pe, S, t):
            pe.wait_ge(S.hf_done, t + 1)
            pe.wait_ge(S.hl_done, t)
            for s in range(2):
                mm = pe.transpose(bank[TURNED_H][:, s * P:s * P + P], hf[:, 0, s * P:s * P + P], ident[:, :])
            mm.then_inc(S.ht_done, 1)

        def pe_step(pe, S, st, e, by_token):
            B, S0, i0 = st["B"], st["S"] + st["n"] * e, st["n"] // 2 * e

            def step(j, m, q):
                pe_gate(pe, S, gate_at(B, m), i0 + q, S0 + j, by_token)
                if by_token:
                    pe_turn_h(pe, S, S0 + j - 1)
                pe_up(pe, S, gate_at(B, m) + 1, i0 + q, S0 + j, by_token)
                pe.wait_ge(S.hl_done, S0 + j)
                pe_rows(pe, S, rows_at(B, m - 1), i0 + q, hh, hl, 1 if by_token else TT)
            return step

        def pe_ffn(pe, st):
            B, n, S0 = st["B"], st["n"], st["S"]
            pe_gate(pe, main, B, 0, S0, False)
            pe_up(pe, main, B + 1, 0, S0, False)
            open_down(pe, 4)
            in_steps(pe, n, pe_step(pe, main, st, 0, False))
            pe.wait_ge(main.hl_done, S0 + n)
            pe_last_rows(pe, B + 3 * n - 1, hh, hl)

        def pe_turn(pe, src, banks, chunks, signal):
            for k in chunks:
                for t in range(TT):
                    o = bank[banks[k // 2]][:, k % 2 * T + t * P:k % 2 * T + t * P + P]
                    mm = pe.transpose(o, src[:, t, k * P:k * P + P], ident[:, :])
                if k % 2 or k == chunks[-1]:
                    mm.then_inc(signal, 1)

        def pe_gather(pe, S, e):
            pe.wait_ge(S.pick_done, 2 * e + 2)
            for g, (src, b) in enumerate(((h2h, 4), (h2h, 5), (h2l, 6), (h2l, 4))):
                if g == 3:
                    pe.wait_ge(S.gh_done, 2 * e + 1)
                for k in range(4):
                    ch = slice((g % 2 * 4 + k) * P, (g % 2 * 4 + k) * P + P)
                    for t in range(TT):
                        mm = pe.matmul(bank[b][:, k * P:k * P + P], src[:, t, ch], pick[:, t, :], start=(t == 0),
                                       stop=(t == 1))
                mm.then_inc(S.gathered, 1)

        def pe_experts(pe, S, st):
            B, n = st["B"], st["n"]
            pe_gather(pe, S, 0)

            def begin(c, i, e):
                pe.wait_ge(S.gh_done, 2 * e + 2)
                pe.wait_ge(S.gl_done, 2 * e + 2)
                pe_gate(pe, S, c, i, st["S"] + n * e, True)
                pe_up(pe, S, c + 1, i, st["S"] + n * e, True)

            def spread(e, b):
                t, h = b // 2, b % 2
                if b == 3:
                    pe.wait_ge(S.added, 4 * e + 2)
                o, half = bank[(4, 5, 6, 4)[b]][:, :], slice(h * 512, h * 512 + 512)
                pe.matmul(o, pickT[:, t * P:t * P + P], yh[:, half], start=True, stop=False)
                pe.matmul(o, pickT[:, t * P:t * P + P], yl[:, half], start=False, stop=True).then_inc(S.spread, 1)

            def step1(e, before=None):
                i0, S0 = n // 2 * e, st["S"] + n * e
                pe_gate(pe, S, gate_at(B, 1), i0, S0 + 1, True)
                pe_turn_h(pe, S, S0)
                if before is not None:
                    for b in range(3):
                        spread(before, b)
                pe_up(pe, S, gate_at(B, 1) + 1, i0, S0 + 1, True)
                if before is not None:
                    spread(before, 3)
                pe.wait_ge(S.hl_done, S0 + 1)
                pe_rows(pe, S, rows_at(B, 0), i0, hh, hl, 1)

            def expert(e, last):
                S0, i0 = st["S"] + n * e, n // 2 * e
                step = pe_step(pe, S, st, e, True)
                with pe.Fori(0, n // 2 - 2) as q:
                    step(2 + 2 * q, 2, q)
                    step(3 + 2 * q, 3, q)
                pe.wait_ge(S.added, 4 * e + 1)
                for t in range(TT):
                    mm = pe.transpose(bank[5][:, t * P:t * P + P], pick[:, t, :].bitcast(F32), ident[:, :])
                mm.then_inc(S.pick_turned, 1)
                step(n - 2, n - 2, 0)
                step(n - 1, n - 1, 0)
                pe.wait_ge(S.pickT_done, e + 1)
                if not last:
                    pe_gather(pe, S, e + 1)
                pe_turn_h(pe, S, S0 + n - 1)
                pe.wait_ge(S.hl_done, S0 + n)
                pe_rows(pe, S, B + 3 * n - 1, i0, hh, hl, 1, last=True)
                if not last:
                    begin(B + 3 * n, i0, e + 1)
                pe.wait_ge(S.yl_done, 2 * e + 2)
                if last:
                    for b in range(4):
                        spread(e, b)
                else:
                    open_down(pe, 2)
                    step1(e + 1, before=e)

            begin(B, 0, 0)
            open_down(pe, 2)
            step1(0)
            with pe.Fori(0, NE - 1) as e:
                expert(e, False)
            expert(NE - 1, True)

        def pe_mix1(pe, st):
            B, l = st["B"], st["layer"]
            for m in range(8):
                n, bk = B + m, MIX1_BANKS[m]
                if m in (2, 3, 4):
                    pe_cols(pe, main, n, 0, bk, T).then_inc(main.multiplied, 1)
                else:
                    pe.wait_ge(main.lo_done, n + 1)
                    pe_toks(pe, n, (bk, bk), FW).then_inc(main.multiplied, 1)
            pe.wait_ge(ev("vn_out"), 2 * (l + 1))
            for t in range(TT):
                for h in range(SH):
                    mm = pe.matmul(bank[t][:, h * P:h * P + P], wsT[:, l, h, :], vn[:, t, h * P:h * P + P],
                                   start=True, stop=True)
                mm.then_inc(ev("sgu_out"), 1)
            pe.wait_ge(ev("pool_in"), l + 1)
            pe.wait_ge(ev("poolw_in"), 64)
            for t in range(TT):
                for c in range(2):
                    mm = pe.matmul(bank[6][:, t * 256 + c * P:t * 256 + c * P + P], dT[:, c, t * P:t * P + P],
                                   poolw[:, l, c, :], start=True, stop=True)
            mm.then_inc(ev("pool_out"), 1)
            pe.wait_ge(ev("conv_in"), l + 1)
            for t in range(TT):
                for c in range(2):
                    mm = pe.transpose(bank[7][:, t * 256 + c * P:t * 256 + c * P + P], zc[:, c, t * P:t * P + P],
                                      ident[:, :])
            mm.then_inc(ev("conv_out"), 1)
            pe.wait_ge(ev("y_ready"), l + 1)
            pe_turn(pe, y1, Y_BANKS, range(KD), ev("y_turned"))
            pe.wait_ge(ev("yl_out"), 8 * (l + 1))
            for m in range(3):
                pe_rows(pe, main, B + 8 + m, 0, xh[:, 2 * m:2 * m + 2, :], xl[:, 2 * m:2 * m + 2, :], TT,
                        first=(m == 0))
            pe_last_rows(pe, B + 11, xh[:, 6:8, :], xl[:, 6:8, :])

        def pe_mix2(pe, st):
            B, l = st["B"], st["layer"]
            for m in range(7):
                n, bk = B + m, MIX2_BANKS[m]
                if m >= 3:
                    pe_cols(pe, main, n, 0, bk, T).then_inc(main.multiplied, 1)
                else:
                    pe.wait_ge(main.lo_done, n + 1)
                    pe_toks(pe, n, (bk, bk), MIX2_COLS[m][1]).then_inc(main.multiplied, 1)
            pe.wait_ge(ev("lat_ready"), l + 1)
            pe_turn(pe, ptok, (5, 0, 1), range(5), ev("lat_turned"))
            pe.wait_ge(ev("latl_out"), 5 * (l + 1))
            pe.wait_ge(ev("u_ready"), l + 1)
            for m, ks in ((7, (0, 1)), (8, (2,))):
                pe.wait_ge(main.lo_done, B + m + 1)
                for h in range(2):
                    mm = pe_toks(pe, B + m, (Q_BANKS[0][h], Q_BANKS[1][h]), 4 * QK, ks, stride=0, first=(m == 7),
                                 last=(m == 8), c0=h * 4 * QK, row=NH * QK)
                mm.then_inc(main.multiplied, 1)
            pe.wait_ge(main.lo_done, B + 10)
            for h in range(2):
                mm = pe_toks(pe, B + 9, (KV_BANKS[0][h], KV_BANKS[1][h]), 512, (3, 4), stride=0, c0=h * 512, row=D)
            mm.then_inc(main.multiplied, 1)
            pe.wait_ge(ev("qk_ready"), l + 1)
            for g in range(8):
                if g >= 4:
                    pe.wait_ge(ev("qkT_out"), 8 * l + g - 3)
                for h in range(2):
                    for t in range(TT):
                        mm = pe.transpose(bank[TURN4[g % 4]][0:QK, h * T + t * P:h * T + t * P + P],
                                          qk[:, t, 2 * g + h, :], ident[:, :])
                mm.then_inc(ev("qk_turned"), 1)
            pe.wait_ge(ev("qkT_out"), 8 * (l + 1))
            for i in range(NH + 2):
                if i < NH:
                    h = i
                    if h >= 2:
                        pe.wait_ge(ev("exp_out"), 16 * l + 2 * (h - 1))
                    pe.matmul(bank[h % 2][:, 0:P], qkT[0:QK, h, 0:P], qkT[0:QK, NH + h, 0:P], start=True, stop=True)
                    pe.matmul(bank[h % 2][:, P:3 * P], qkT[0:QK, h, P:T], qkT[0:QK, NH + h, :], start=True,
                              stop=True).then_inc(ev("score_out"), 1)
                if 1 <= i <= NH:
                    h = i - 1
                    pe.wait_ge(ev("exp_out"), 16 * l + 2 * (h + 1))
                    if h >= 2:
                        pe.wait_ge(ev("probT_out"), 8 * l + h - 1)
                    for b in range(3):
                        mm = pe.transpose(bank[4 + h % 2][:, b * P:b * P + P], prob[:, h % 2, b * P:b * P + P],
                                          ident[:, :])
                    mm.then_inc(ev("prob_turned"), 1)
                if i >= 2:
                    h = i - 2
                    pe.wait_ge(ev("probT_out"), 8 * l + h + 1)
                    pe.matmul(bank[6][:, h * VD:h * VD + VD], probT[:, h % 2, 0:P], v2[:, 0, h, :], start=True,
                              stop=True)
                    pe.matmul(bank[7][:, h * VD:h * VD + VD], probT[:, h % 2, P:T], v2[:, 0, h, :], start=True,
                              stop=False)
                    pe.matmul(bank[7][:, h * VD:h * VD + VD], probT[:, h % 2, T:3 * P], v2[:, 1, h, :], start=False,
                              stop=True).then_inc(ev("att_out"), 1)
            pe.wait_ge(ev("conv31_out"), l + 1)
            for t in range(TT):
                for c in range(4):
                    mm = pe.transpose(bank[2 + t][:, c * P:c * P + P], acc[:, c, t * P:t * P + P], ident[:, :])
            mm.then_inc(ev("c_turned"), 1)
            pe.wait_ge(ev("att_ready"), l + 1)
            pe_turn(pe, xn, CAT_BANKS, range(4), ev("cat_turned"))
            pe.wait_ge(ev("c_ready"), l + 1)
            pe_turn(pe, xn, CAT_BANKS, range(4, 8), ev("cat_turned"))
            pe.wait_ge(ev("catl_out"), 3 * (l + 1))
            for m in range(3):
                pe_rows(pe, main, B + 10 + m, 0, xh[:, 2 * m:2 * m + 2, :], xl[:, 2 * m:2 * m + 2, :], TT,
                        first=(m == 0))
            pe_last_rows(pe, B + 13, xh[:, 6:8, :], xl[:, 6:8, :])

        def pe_router(pe):
            pe.wait_ge(ev("rwl_out"), 1)
            for t in range(TT):
                for k in range(KD):
                    for n, (a, b) in enumerate(((xh, rwh), (xh, rwl), (xl, rwh), (xl, rwl))):
                        mm = pe.matmul(bank[6][:, t * NE:t * NE + NE], a[:, k, t * P:t * P + P], b[:, k, :],
                                       start=(k == 0 and n == 0), stop=(k == KD - 1 and n == 3))
            mm.then_inc(ev("logit_out"), 1)
            pe.wait_ge(ev("sel_out"), 1)
            pe.matmul(bank[7][:, 0:NE], before[:, :], sel[:, 0, :], start=True, stop=True)
            pe.matmul(bank[7][:, NE:2 * NE], ones[:, :], sel[:, 0, :], start=True, stop=False)
            pe.matmul(bank[7][:, NE:2 * NE], before[:, :], sel[:, 1, :], start=False, stop=True)
            pe.matmul(bank[7][:, 2 * NE:3 * NE], ones[:, :], sel[:, 0, :], start=True, stop=False)
            pe.matmul(bank[7][:, 2 * NE:3 * NE], ones[:, :], sel[:, 1, :], start=False, stop=True)\
              .then_inc(ev("count_out"), 1)

        def pe_constants(pe):
            pe.wait_ge(ev("rows_in"), 16 * len(staged[::2]))
            pe.wait_ge(ev("odd_rows_in"), 16 * len(staged[1::2]))
            for tile, n in enumerate(used):
                pe.transpose(bank[6][:, tile * P:tile * P + n], stage_rows[0:n, tile, :],
                             ident[0:n, 0:n]).then_inc(ev("chan_turned"), 1)
            pe.wait_ge(ev("ws_in"), 16)
            for l in range(2):
                for h in range(SH):
                    mm = pe.transpose(bank[(7, 1)[l]][:, h * P:h * P + P], stage_ws[:, l, h, :], ident[:, :])
                mm.then_inc(ev("ws_turned"), 1)
            pe.wait_ge(ev("const_pool"), N_POOL)
            pe.wait_ge(ev("const_vec"), N_VEC)

        @block.tensor
        def _(pe):
            pe.wait_ge(ev("ident_out"), 1)
            for st in stages:
                k = st["kind"]
                if k == "post":
                    continue
                for b in range(4):
                    pe.wait_ge(xn_done, 4 * st["M"] + b + 1)
                    for n in range(4):
                        mm = pe.transpose(bank[DOWN[b]][:, n * P:n * P + P],
                                          xn[:, b // 2, (b % 2 * 4 + n) * P:(b % 2 * 4 + n) * P + P], ident[:, :])
                    mm.then_inc(turned, 1)
                if st["M"] == 0:
                    pe_constants(pe)
                pe.wait_ge(xl_done, 4 * (st["M"] + 1))
                if k == "mix1":
                    pe_mix1(pe, st)
                elif k == "mix2":
                    pe_mix2(pe, st)
                elif k == "moe":
                    pe_router(pe)
                    pe.wait_ge(ev("h2l_out"), 2)
                    pe_experts(pe, main, st)
                    pe.wait_ge(ev("spill_known"), 1)
                    flag = pe.value_load(spill[0:1, 0:1])
                    with pe.If(flag > 0):
                        pe.wait_ge(main.added, 4 * NE + 1)
                        pe.wait_ge(ev("spill_set"), 1)
                        pe_experts(pe, again, SPILL)
                        pe.wait_ge(again.added, 4 * NE + 1)
                        pe.nop()
                    pe.end_ifs()
                else:
                    pe_ffn(pe, st)

        @block.gpsimd
        def _(pool):
            g = nc.gpsimd
            n = 0

            def link(ins):
                nonlocal n
                n += 1
                ins.then_inc(pchain, 1)
                pool.wait_ge(pchain, n)

            def load_gain(q):
                pool.dma_start(gains[:, q % 2, :], gain_of(stages[q]).partition_broadcast(P)).then_inc(gain_in[q % 2], 16)

            load_gain(0)
            load_gain(1)
            link(g.memset(ident[:], 0.0))
            g.affine_select(out=ident[:], in_=ident[:], compare_op=ALU.not_equal, fill=1.0, base=0,
                            pattern=[[-1, P]], channel_multiplier=1).then_inc(ev("ident_out"), 1)
            for tile, at, rows, ap in staged[1::2]:
                pool.dma_start(stage_rows[at:at + rows, tile, :], ap).then_inc(ev("odd_rows_in"), 16)
            pool.dma_start(stage_ws[:], A["sgu_w"].rearrange("l h i j -> i l h j")).then_inc(ev("ws_in"), 16)
            link(g.memset(ones[:], 1.0))
            link(g.memset(poolw[:], 0.0))
            g.affine_select(out=before[:], in_=ones[:], compare_op=ALU.is_gt, fill=0.0, base=0,
                            pattern=[[1, P]], channel_multiplier=-1).then_inc(ev("const_pool"), 1)
            g.iota(slots[:], pattern=[[1, P]], base=0, channel_multiplier=0,
                   allow_small_or_imprecise_dtypes=True).then_inc(ev("const_pool"), 1)
            g.iota(invc[:], pattern=[[0, 2], [1, T]], base=1, channel_multiplier=0,
                   allow_small_or_imprecise_dtypes=True).then_inc(ev("const_pool"), 1)
            g.affine_select(out=earlier[:], in_=ones[:, 0:NE * NE].rearrange("p (e j) -> p e j", e=NE),
                            compare_op=ALU.is_gt, fill=0.0, base=0, pattern=[[1, NE], [-1, NE]],
                            channel_multiplier=0).then_inc(ev("const_pool"), 1)
            small = [
                (ropet[:], rope.rearrange("(t p) c -> p t c", p=P)),
                (lng[:], A["sgu_ln_g"][0].partition_broadcast(P)),
                (lnb[:], A["sgu_ln_b"][0].partition_broadcast(P)),
                (psc[:], A["pool_scale"][0].partition_broadcast(P)),
                (qkg[:, :, 0, :], A["q_norm_2"].partition_broadcast(P)),
                (qkg[:, :, 1, :], A["k_norm_2"].partition_broadcast(P)),
                (routw[:], A["router_w"][0].rearrange("(k p) e -> p k e", p=P)),
                (routb[:], A["router_b"][0].partition_broadcast(P)),
            ]
            assert len(small) == N_SMALL
            for dst, src in small:
                pool.dma_start(dst, src).then_inc(ev("small_in"), 16)
            for r in range(2):
                for l in range(2):
                    pool.dma_start(poolw[64 * r:64 * r + 64, l, :, 64 * r:64 * r + 64],
                                  A["pool_w"][l, r::2].rearrange("c i o -> i c o")).then_inc(ev("poolw_in"), 16)
            pool.wait_ge(ev("y_raw"), 1)
            for dst, name in ((lng, "sgu_ln_g"), (lnb, "sgu_ln_b"), (psc, "pool_scale")):
                pool.dma_start(dst[:], A[name][1].partition_broadcast(P)).then_inc(ev("small1_in"), 16)
            for q in range(2, len(stages)):
                pool.wait_ge(ssq_done, TT * q)
                load_gain(q)

        @block.vector
        def _(dve):
            v = nc.vector
            count = [0]

            def note(ins):
                count[0] += 1
                ins.then_inc(chain, 1)

            def settle():
                dve.wait_ge(chain, count[0])

            def link(ins):
                note(ins)
                settle()

            marks = [0]

            def mark(s, inc=1):
                v.memset(touch[:, marks[0]:marks[0] + 1], 0.0).then_inc(s, inc)
                marks[0] += 1

            def lo_piece(S, c, i, n=PIECE):
                dve.wait_ge(S.hi_done, c + 1 + 6 * i)
                v.tensor_tensor(lo[:, c % RING, 0:n], raw[:, c % RING, 0:n], hi[:, c % HRING, 0:n].bitcast(F32),
                                ALU.subtract).then_inc(S.lo_done, 1)

            def hidden(S, c, i, t, by_token):
                dve.wait_ge(S.sg_done, t + 1)
                dve.wait_ge(S.multiplied, c + 1 + 6 * i)
                dve.wait_ge(S.hl_done, t)
                if by_token:
                    o, a, b = hf[:, 0, :], sg[:, 0, :], bank[UP][:, 0:FW]
                else:
                    o, a, b = hf[:, :, :], sg[:, :, :], whole(bank[UP])
                v.tensor_tensor(o, a, b, ALU.mult).then_inc(S.hf_done, 1)

            def rest_h(S, t, by_token):
                dve.wait_ge(S.hh_done, t + 1)
                a, w = (turned_h(), P) if by_token else (hf[:, :, :], T)
                v.tensor_tensor(hl[:, :, 0:w], a, hh[:, :, 0:w].bitcast(F32), ALU.subtract).then_inc(S.hl_done, 1)

            def step_of(S, st, e, by_token):
                B, S0, i0 = st["B"], st["S"] + st["n"] * e, st["n"] // 2 * e

                def step(j, m, q):
                    lo_piece(S, gate_at(B, m), i0 + q)
                    hidden(S, gate_at(B, m - 1) + 1, i0 + q, S0 + j - 1, by_token)
                    lo_piece(S, gate_at(B, m) + 1, i0 + q)
                    lo_piece(S, rows_at(B, m - 1), i0 + q)
                    rest_h(S, S0 + j - 1, by_token)
                return step

            def ffn(st):
                B, n, S0 = st["B"], st["n"], st["S"]
                in_steps(dve, n, step_of(main, st, 0, False))
                hidden(main, gate_at(B, n - 1) + 1, 0, S0 + n - 1, False)
                lo_piece(main, B + 3 * n - 1, 0)
                rest_h(main, S0 + n - 1, False)

            def ahead(st):
                lo_piece(main, st["B"], 0)
                lo_piece(main, st["B"] + 1, 0)

            def norm(st):
                q, g, post = st["Q"], gains[:, st["Q"] % 2, :], st["kind"] == "post"
                for t in range(TT):
                    dve.wait_ge(ssq_done, TT * q + t + 1)
                    v.tensor_scalar(var[:, t:t + 1], ssq[:, t:t + 1], 1.0 / D, EPS, ALU.mult,
                                    ALU.add).then_inc(var_done, 1)
                dve.wait_ge(gain_in[q % 2], 16 * (q // 2 + 1))
                for t in range(TT):
                    dve.wait_ge(std_done, TT * q + t + 1)
                    link(v.reciprocal(rstd[:, t:t + 1], std[:, t:t + 1]))
                    if post:
                        v.scalar_tensor_tensor(x[:, t, :], x[:, t, :], rstd[:, t:t + 1], g, ALU.mult,
                                               ALU.mult).then_inc(x_done, 1)
                        continue
                    for h in range(2):
                        half = slice(h * 512, h * 512 + 512)
                        v.scalar_tensor_tensor(xn[:, t, half], x[:, t, half], rstd[:, t:t + 1], g[:, half], ALU.mult,
                                               ALU.mult).then_inc(xn_done, 1)
                if not post:
                    for b in range(4):
                        dve.wait_ge(xh_done, 4 * st["M"] + b + 1)
                        v.tensor_tensor(norm_part(xl, b), norm_bank(b), norm_part(xh, b).bitcast(F32),
                                        ALU.subtract).then_inc(xl_done, 1)

            def add_down(st, factor, end):
                if after(st):
                    ahead(after(st))
                dve.wait_ge(first_tile, st["W"] + 1)
                for b in range(4):
                    if b == 2:
                        dve.wait_ge(main.multiplied, end)
                    xs = x[:, b // 2, b % 2 * 512:b % 2 * 512 + 512]
                    ins = v.scalar_tensor_tensor(xs, bank[DOWN[b]][:, :], factor, xs, ALU.mult, ALU.add)
                    if b % 2:
                        ins.then_inc(x_done, 1)

            def turned_rest(dst, src, gain, high, signal):
                v.scalar_tensor_tensor(dst, src, gain, high.bitcast(F32), ALU.mult, ALU.subtract).then_inc(signal, 1)

            def mix1(st):
                B, l = st["B"], st["layer"]
                v.memset(apad[:, :, 0:PAD], 0.0).then_inc(ev("pads"), 1)
                link(v.memset(zpad[:, :, 0:CW - 1], 0.0))
                for m in range(2, 5):
                    lo_piece(main, B + m, 0)
                dve.wait_ge(main.multiplied, B + 2)
                for t in range(TT):
                    for b in range(2):
                        note(v.bn_stats(bns[:, t, b, :], bank[b][:, t * 256:t * 256 + 256]))
                settle()
                for t in range(TT):
                    note(v.bn_aggr(bna[:, t, :], bns[:, t, :, :]))
                settle()
                v.tensor_scalar(var[:, 2:4], bna[:, :, 1], EPS, None, ALU.add).then_inc(ev("v_var"), 1)
                lo_piece(main, B + 5, 0)
                lo_piece(main, B + 6, 0)
                dve.wait_ge(ev("v_std"), l + 1)
                link(v.reciprocal(rstd[:, 2:4], std[:, 2:4]))
                for t in range(TT):
                    for b in range(2):
                        note(v.tensor_scalar(vn[:, t, b * 256:b * 256 + 256], bank[b][:, t * 256:t * 256 + 256],
                                             bna[:, t, 0:1], rstd[:, 2 + t:3 + t], ALU.subtract, ALU.mult))
                settle()
                if l == 0:
                    dve.wait_ge(ev("small_in"), 16 * N_SMALL)
                else:
                    dve.wait_ge(ev("small1_in"), 48)
                for t in range(TT):
                    note(v.tensor_tensor(vn[:, t, :], vn[:, t, :], lng[:, :], ALU.mult))
                settle()
                for t in range(TT):
                    v.tensor_tensor(vn[:, t, :], vn[:, t, :], lnb[:, :], ALU.add).then_inc(ev("vn_out"), 1)
                lo_piece(main, B + 7, 0)
                dve.wait_ge(ev("a_out"), l + 1)
                N = PAD + T
                link(v.tensor_tensor(w2[:, :, 1:N], apad[:, :, 1:N], apad[:, :, 0:N - 1], ALU.add))
                link(v.tensor_tensor(w4[:, :, 3:N], w2[:, :, 3:N], w2[:, :, 1:N - 2], ALU.add))
                link(v.tensor_tensor(w8[:, 1, 7:N], w4[:, 1, 7:N], w4[:, 1, 3:N - 4], ALU.add))
                link(v.tensor_tensor(w16[:, 1, 15:N], w8[:, 1, 15:N], w8[:, 1, 7:N - 8], ALU.add))
                for g, wsum in enumerate((w2, w4, w8, w16)):
                    pr, c = slice(g % 2 * 64, g % 2 * 64 + 64), g // 2
                    note(v.tensor_tensor(dT[pr, c, :], wsum[pr, c, PAD:N], invc[pr, c, :], ALU.mult))
                settle()
                v.tensor_tensor(dT[:, :, :], dT[:, :, :], apad[:, :, PAD:N], ALU.subtract).then_inc(ev("pool_in"), 1)
                dve.wait_ge(ev("gc_out"), l + 1)
                dve.wait_ge(main.multiplied, B + 5)
                link(v.tensor_tensor(zpad[:, :, CW - 1:], gcT[:, :, :], bank[2][:, :].rearrange(
                    "p (c t) -> p c t", c=2), ALU.mult))
                for c in range(2):
                    note(v.tensor_scalar(zc[:, c, :], zpad[:, c, 0:T], col(("cw", l), c), None, ALU.mult))
                settle()
                for k in range(1, CW):
                    for c in range(2):
                        ins = v.scalar_tensor_tensor(zc[:, c, :], zpad[:, c, k:k + T], col(("cw", l), 2 * k + c),
                                                     zc[:, c, :], ALU.mult, ALU.add)
                        note(ins)
                    settle()
                mark(ev("conv_in"))
                for m in range(8, 11):
                    lo_piece(main, B + m, 0)
                dve.wait_ge(ev("sgu_out"), 2 * (l + 1))
                dve.wait_ge(ev("u_out"), 2 * (l + 1))
                for t in range(TT):
                    for h in range(SH):
                        v.scalar_tensor_tensor(y1[:, t, DP + h * P:DP + h * P + P], bank[t][:, h * P:h * P + P],
                                               col(("sb", l), h), u1[:, t, h * P:h * P + P], ALU.add, ALU.mult)
                dve.wait_ge(ev("pool_out"), l + 1)
                for t in range(TT):
                    v.tensor_tensor(y1[:, t, 0:DP], bank[6][:, t * 256:t * 256 + 256], psc[:, :], ALU.mult)
                dve.wait_ge(ev("conv_out"), l + 1)
                dve.wait_ge(ev("gb_out"), l + 1)
                for t in range(TT):
                    ins = v.tensor_tensor(y1[:, t, DP + DS:D], gb[:, t, :], bank[7][:, t * 256:t * 256 + 256], ALU.mult)
                ins.then_inc(ev("y_raw"), 1)
                dve.wait_ge(ev("y_sq"), 6 * (l + 1))
                sums = ssq[:, 2:8].rearrange("p (t g) -> p t g", t=2)
                vars_ = var[:, 2:8].rearrange("p (t g) -> p t g", t=2)
                for g, n in enumerate((DP, DS, DC)):
                    ins = v.tensor_scalar(vars_[:, :, g], sums[:, :, g], 1.0 / n, EPS, ALU.mult, ALU.add)
                ins.then_inc(ev("y_var"), 1)
                dve.wait_ge(ev("y_std"), l + 1)
                link(v.reciprocal(rstd[:, 2:8], std[:, 2:8]))
                for t in range(TT):
                    for g, (c0, c1) in enumerate(((0, DP), (DP, DP + DS), (DP + DS, D))):
                        ins = v.tensor_scalar(y1[:, t, c0:c1], y1[:, t, c0:c1], rstd[:, 2 + 3 * t + g:3 + 3 * t + g],
                                              None, ALU.mult)
                ins.then_inc(ev("y_ready"), 1)
                for k in range(KD):
                    dve.wait_ge(ev("yh_out"), 8 * l + bank_end(k, KD))
                    turned_rest(xl[:, k, :], bank[Y_BANKS[k // 2]][:, k % 2 * T:(k % 2 + 1) * T],
                                col(("group", l), k), xh[:, k, :], ev("yl_out"))
                lo_piece(main, B + 11, 0)
                add_down(st, 1.0, B + MIX1_PIECES)

            def router(st):
                lo_router = v.tensor_tensor
                dve.wait_ge(ev("rwh_out"), 1)
                lo_router(rwl[:], routw[:], rwh[:].bitcast(F32), ALU.subtract).then_inc(ev("rwl_out"), 1)
                for t in range(TT):
                    dve.wait_ge(ev("h2h_out"), t + 1)
                    v.tensor_tensor(h2l[:, t, :], xn[:, t, :], h2h[:, t, :].bitcast(F32),
                                    ALU.subtract).then_inc(ev("h2l_out"), 1)
                dve.wait_ge(ev("logit_out"), 1)
                for t in range(TT):
                    note(v.tensor_tensor(logit[:, t, :], bank[6][:, t * NE:t * NE + NE], routb[:, :], ALU.add))
                settle()
                for t in range(TT):
                    mine = logit[:, t, :].unsqueeze(2).to_broadcast([P, NE, NE])
                    other = logit[:, t, :].unsqueeze(1).to_broadcast([P, NE, NE])
                    b1 = big[:, t, :].rearrange("p (e j) -> p e j", e=NE)
                    b2 = big2[:, t, :].rearrange("p (e j) -> p e j", e=NE)
                    note(v.tensor_tensor(b1, other, mine, ALU.is_gt))
                    note(v.tensor_tensor(b2, other, mine, ALU.is_equal))
                    settle()
                    link(v.tensor_tensor(b2, b2, earlier[:, :, :], ALU.mult))
                    link(v.tensor_tensor(b1, b1, b2, ALU.add))
                    note(v.tensor_reduce(place[:, t, :], b1, AX, ALU.add))
                    note(v.tensor_reduce(top[:, t:t + 1], logit[:, t, :], AX, ALU.max))
                settle()
                v.tensor_scalar(sel[:], place[:], float(2), None, ALU.is_lt).then_inc(ev("sel_out"), 1)
                for t in range(TT):
                    ins = v.tensor_scalar(ex[:, t, :], logit[:, t, :], top[:, t:t + 1], None, ALU.subtract)
                ins.then_inc(ev("shifted"), 1)
                dve.wait_ge(ev("ex_out"), 1)
                link(v.tensor_tensor(gates[:], ex[:], sel[:], ALU.mult))
                link(v.tensor_reduce(den[:, :], gates[:], AX, ALU.add))
                link(v.reciprocal(rden[:, :], den[:, :]))
                for t in range(TT):
                    note(v.tensor_scalar(gates[:, t, :], gates[:, t, :], rden[:, t:t + 1], None, ALU.mult))
                settle()
                dve.wait_ge(ev("count_out"), 1)
                note(v.memset(rank[:], -1.0))
                settle()
                for t in range(TT):
                    note(v.scalar_tensor_tensor(rank[:, t, 0, 0:NE], bank[7][:, t * NE:t * NE + NE], 1.0, sel[:, t, :],
                                                ALU.add, ALU.mult))
                note(v.tensor_reduce(most[:, :], bank[7][:, 2 * NE:3 * NE], AX, ALU.max))
                settle()
                for t in range(TT):
                    note(v.tensor_scalar(rank[:, t, 1, 0:NE], rank[:, t, 0, 0:NE], -1.0 - P, None, ALU.add))
                settle()
                for t in range(TT):
                    note(v.tensor_scalar(rank[:, t, 0, 0:NE], rank[:, t, 0, 0:NE], -1.0, None, ALU.add))
                settle()
                v.tensor_scalar(spill[0:1, 0:1], most[0:1, 0:1], float(P), None, ALU.is_gt).then_inc(ev("spill_known"), 1)

            def pick_of(S, pass_, e):
                for t in range(TT):
                    v.tensor_scalar(pick[:, t, :], slots[:, :], rank[:, t, pass_, bass.ds(e, 1)], None,
                                    ALU.is_equal).then_inc(S.pick_done, 1)

            def gathered_rest(S, e):
                for b in range(2):
                    dve.wait_ge(S.gathered, 4 * e + b + 3)
                    v.tensor_copy(xl[:, 4 * b:4 * b + 4, 0:P], bank[(6, 4)[b]][:, :].rearrange(
                        "p (k s) -> p k s", k=4)).then_inc(S.gl_done, 1)

            def experts(S, st, pass_):
                B, n = st["B"], st["n"]
                pick_of(S, pass_, 0)
                gathered_rest(S, 0)
                if S is again:
                    lo_piece(S, B, 0)
                    lo_piece(S, B + 1, 0)
                step_of(S, st, 0, True)(1, 1, 0)

                def add(e, b):
                    dve.wait_ge(S.spread, 4 * e + b + 1)
                    xs = x[:, b // 2, b % 2 * 512:b % 2 * 512 + 512]
                    v.scalar_tensor_tensor(xs, bank[(4, 5, 6, 4)[b]][:, :], gates[:, b // 2, bass.ds(e, 1)], xs,
                                           ALU.mult, ALU.add).then_inc(S.added, 1)

                def expert(e, last):
                    S0, i0 = st["S"] + n * e, n // 2 * e
                    step = step_of(S, st, e, True)
                    with dve.Fori(0, n // 2 - 2) as q:
                        step(2 + 2 * q, 2, q)
                        step(3 + 2 * q, 3, q)
                    step(n - 2, n - 2, 0)
                    if not last:
                        dve.wait_ge(S.pick_turned, e + 1)
                        pick_of(S, pass_, e + 1)
                    step(n - 1, n - 1, 0)
                    hidden(S, gate_at(B, n - 1) + 1, i0, S0 + n - 1, True)
                    lo_piece(S, B + 3 * n - 1, i0)
                    if not last:
                        lo_piece(S, B + 3 * n, i0)
                        gathered_rest(S, e + 1)
                    rest_h(S, S0 + n - 1, True)
                    if not last:
                        lo_piece(S, B + 3 * n + 1, i0)
                    for b in range(2):
                        dve.wait_ge(S.yh_done, 2 * e + b + 1)
                        v.tensor_tensor(yl[:, 512 * b:512 * b + 512], bank[2 + b][:, :],
                                        yh[:, 512 * b:512 * b + 512].bitcast(F32), ALU.subtract).then_inc(S.yl_done, 1)
                    if last:
                        for b in range(4):
                            add(e, b)
                        return
                    i1 = n // 2 * (e + 1)
                    lo_piece(S, gate_at(B, 1), i1)
                    hidden(S, B + 1, i1, S0 + n, True)
                    lo_piece(S, gate_at(B, 1) + 1, i1)
                    for b in range(3):
                        add(e, b)
                    lo_piece(S, rows_at(B, 0), i1)
                    rest_h(S, S0 + n, True)
                    add(e, 3)

                with dve.Fori(0, NE - 1) as e:
                    expert(e, False)
                expert(NE - 1, True)

            def mix2(st):
                B, l = st["B"], st["layer"]
                link(v.memset(upad[:, :, 0:CPAD], 0.0))
                for m in range(2, 7):
                    lo_piece(main, B + m, 0, KD * MIX2_COLS[m][1])
                dve.wait_ge(ev("lat_sq"), 4 * (l + 1))
                sums = ssq[:, 2:6].rearrange("p (t g) -> p t g", t=2)
                vars_ = var[:, 2:6].rearrange("p (t g) -> p t g", t=2)
                for g, n in enumerate((QL, KVL)):
                    ins = v.tensor_scalar(vars_[:, :, g], sums[:, :, g], 1.0 / n, EPS, ALU.mult, ALU.add)
                ins.then_inc(ev("lat_var"), 1)
                dve.wait_ge(ev("lat_std"), l + 1)
                link(v.reciprocal(rstd[:, 2:6], std[:, 2:6]))
                for t in range(TT):
                    for g, (c0, c1) in enumerate(((0, QL), (QL, QL + KVL))):
                        ins = v.tensor_scalar(ptok[:, t, c0:c1], ptok[:, t, c0:c1], rstd[:, 2 + 2 * t + g:3 + 2 * t + g],
                                              None, ALU.mult)
                ins.then_inc(ev("lat_ready"), 1)
                lo_piece(main, B + 7, 0, 2 * NH * QK)
                for i in range(2):
                    dve.wait_ge(ev("sig_out"), 2 * l + i + 1)
                    ins = v.tensor_tensor(upad[:, 2 * i:2 * i + 2, CPAD:], acc[:, 2 * i:2 * i + 2, :],
                                          bank[(7, 2)[i]][:, :].rearrange("p (c t) -> p c t", c=2), ALU.mult)
                ins.then_inc(ev("u_ready"), 1)
                lo_piece(main, B + 8, 0, NH * QK)
                lo_piece(main, B + 9, 0)
                for c in range(5):
                    dve.wait_ge(ev("lath_out"), 5 * l + bank_end(c, 5))
                    g = col(("ql", l), c) if c < 3 else col(("kvl", l), c - 3)
                    turned_rest(xl[:, c, :], bank[(5, 0, 1)[c // 2]][:, c % 2 * T:(c % 2 + 1) * T], g, xh[:, c, :],
                                ev("latl_out"))
                taps = [(k, c) for k in range(CK) for c in range(4)]

                def conv(n):
                    for _ in range(n):
                        if not taps:
                            return
                        k, c = taps.pop(0)
                        w = col(("cw2", l), 4 * k + c)
                        if k == 0:
                            if c == 0:
                                dve.wait_ge(ev("u_ready"), l + 1)
                            note(v.tensor_scalar(acc[:, c, :], upad[:, c, 0:T], w, col(("cb", l), c), ALU.mult, ALU.add))
                        else:
                            dve.wait_ge(chain, tap_at[c])
                            note(v.scalar_tensor_tensor(acc[:, c, :], upad[:, c, k:k + T], w, acc[:, c, :], ALU.mult,
                                                        ALU.add))
                        tap_at[c] = count[0]

                tap_at = [0] * 4
                conv(16)
                dve.wait_ge(main.multiplied, B + 10)
                for t in range(TT):
                    note(v.tensor_copy(qk[:, t, NH:2 * NH, NOPE:QK],
                                       ptok[:, t, QL + KVL:TOKW].unsqueeze(1).to_broadcast([P, NH, ROPE])))
                    for h in range(2):
                        kv = bank[KV_BANKS[t][h]][:, :].rearrange("p (h d) -> p h d", h=4)
                        note(v.tensor_copy(qk[:, t, NH + 4 * h:NH + 4 * h + 4, 0:NOPE], kv[:, :, 0:NOPE]))
                        ins = v.tensor_copy(v2[:, t, 4 * h:4 * h + 4, :], kv[:, :, NOPE:])
                        if (t, h) == (1, 1):
                            ins.then_inc(ev("k_out"), 1)
                for m in range(10, 13):
                    lo_piece(main, B + m, 0)
                dve.wait_ge(ev("qk_sq"), l + 1)
                link(v.tensor_reduce(hsq[:, :], sq2[:].rearrange("p t h d -> p (t h) d"), AX, ALU.add))
                v.tensor_scalar(hvar[:, :], hsq[:, :], 1.0 / QK, EPS, ALU.mult, ALU.add).then_inc(ev("qk_var"), 1)
                dve.wait_ge(ev("qk_std"), l + 1)
                link(v.reciprocal(hrstd[:, :], hstd[:, :]))
                qkf = qk[:].rearrange("p t h d -> p (t h) d")
                link(v.tensor_tensor(qkf, qkf, hrstd[:, :].unsqueeze(2).to_broadcast([P, TT * 2 * NH, QK]), ALU.mult))
                for t in range(TT):
                    for g in range(2):
                        hs = qk[:, t, NH * g:NH * g + NH, :]
                        note(v.tensor_tensor(hs, hs, qkg[:, l, g, :].unsqueeze(1).to_broadcast([P, NH, QK]), ALU.mult))
                settle()
                half = ROPE // 2
                for t in range(TT):
                    xa, xb = qk[:, t, :, NOPE:NOPE + half], qk[:, t, :, NOPE + half:QK]
                    cos = ropet[:, t, 0:half].unsqueeze(1).to_broadcast([P, 2 * NH, half])
                    sin = ropet[:, t, half:ROPE].unsqueeze(1).to_broadcast([P, 2 * NH, half])
                    for n, (a, b) in enumerate(((xa, cos), (xb, sin), (xa, sin), (xb, cos))):
                        note(v.tensor_tensor(rt[:, n, t, :, :], a, b, ALU.mult))
                settle()
                for t in range(TT):
                    xa, xb = qk[:, t, :, NOPE:NOPE + half], qk[:, t, :, NOPE + half:QK]
                    v.tensor_tensor(xa, rt[:, 0, t, :, :], rt[:, 1, t, :, :], ALU.subtract)
                    ins = v.tensor_tensor(xb, rt[:, 2, t, :, :], rt[:, 3, t, :, :], ALU.add)
                ins.then_inc(ev("qk_ready"), 1)
                conv(16)
                for i in range(NH + 1):
                    if i < NH:
                        h = i
                        dve.wait_ge(ev("score_out"), 8 * l + h + 1)
                        b = bank[h % 2]
                        note(v.memset(b[0:64, 64:P], NEG))
                        note(v.memset(b[0:64, P + 192:P + T], NEG))
                        settle()
                        note(v.tensor_reduce(nmax[:, 2 * h:2 * h + 1], b[:, 0:P], AX, ALU.max))
                        note(v.tensor_reduce(nmax[:, 2 * h + 1:2 * h + 2], b[:, P:3 * P], AX, ALU.max))
                        settle()
                        v.tensor_scalar(negm[:, 2 * h:2 * h + 2], nmax[:, 2 * h:2 * h + 2], -SCALE, None,
                                        ALU.mult).then_inc(ev("neg_max"), 1)
                    if i >= 1:
                        h = i - 1
                        dve.wait_ge(ev("prob_turned"), 8 * l + h + 1)
                        if h >= 2:
                            dve.wait_ge(ev("att_out"), 8 * l + h - 1)
                        v.tensor_copy(probT[:, h % 2, :], bank[4 + h % 2][:, 0:3 * P]).then_inc(ev("probT_out"), 1)
                    conv(12)
                conv(len(taps))
                settle()
                mark(ev("conv31_out"))
                dve.wait_ge(ev("att_out"), 8 * (l + 1))
                link(v.reciprocal(rsum[:].rearrange("p t h -> p (t h)"), psum_p[:, :]))
                for t in range(TT):
                    ins = v.tensor_tensor(xn[:, t, 0:512].rearrange("p (h d) -> p h d", h=NH),
                                          bank[6 + t][:, :].rearrange("p (h d) -> p h d", h=NH),
                                          rsum[:, t, :].unsqueeze(2).to_broadcast([P, NH, VD]), ALU.mult)
                ins.then_inc(ev("att_ready"), 1)
                dve.wait_ge(ev("c_turned"), l + 1)
                for t in range(TT):
                    note(v.bn_stats(bns[:, t, 0, :], bank[2 + t][:, :]))
                settle()
                for t in range(TT):
                    note(v.bn_aggr(bna[:, t, :], bns[:, t, 0, :]))
                settle()
                v.tensor_scalar(var[:, 2:4], bna[:, :, 1], EPS, None, ALU.add).then_inc(ev("c_var"), 1)
                dve.wait_ge(ev("c_std"), l + 1)
                link(v.reciprocal(rstd[:, 2:4], std[:, 2:4]))
                for t in range(TT):
                    ins = v.tensor_scalar(xn[:, t, 512:1024], bank[2 + t][:, :], bna[:, t, 0:1], rstd[:, 2 + t:3 + t],
                                          ALU.subtract, ALU.mult)
                ins.then_inc(ev("c_ready"), 1)
                for b in range(2):
                    dve.wait_ge(ev("cath_out"), 3 * l + b + 1)
                    v.tensor_tensor(xl[:, 2 * b:2 * b + 2, :], bank[CAT_BANKS[b]][:, :].rearrange(
                        "p (c t) -> p c t", c=2), xh[:, 2 * b:2 * b + 2, :].bitcast(F32),
                        ALU.subtract).then_inc(ev("catl_out"), 1)
                dve.wait_ge(ev("cath_out"), 3 * (l + 1))
                v.tensor_tensor(xl[:, 4:8, :], acc[:, :, :], xh[:, 4:8, :].bitcast(F32),
                                ALU.subtract).then_inc(ev("catl_out"), 1)
                lo_piece(main, B + 13, 0)
                add_down(st, 1.0, B + MIX2_PIECES)

            def constants():
                v.memset(zeros[:].bitcast(F32), 0.0).then_inc(ev("const_vec"), 1)
                for s, n in ((again.hi_done, RING), (again.lo_done, RING), (again.multiplied, RING),
                             (again.sg_done, 1), (again.hf_done, 1), (again.hh_done, 1), (again.hl_done, 1),
                             (again.added, 1), (main.added, 1)):
                    mark(s, n)
                for s in range(RING):
                    mark(again.raw_full[s], 16)
                mark(ev("spill_set"))
                dve.wait_ge(ev("const_pool"), N_POOL)
                for g, w in enumerate(WINDOWS):
                    pr, c = slice(g % 2 * 64, g % 2 * 64 + 64), g // 2
                    note(v.tensor_scalar(invc[pr, c, :], invc[pr, c, :], float(w), None, ALU.min))
                settle()
                note(v.reciprocal(invc[:], invc[:]))
                for tile, n in enumerate(used):
                    dve.wait_ge(ev("chan_turned"), len(used))
                    v.tensor_copy(chan[:, tile, 0:n], bank[6][:, tile * P:tile * P + n]).then_inc(ev("chan_out"), 1)
                for l in range(2):
                    dve.wait_ge(ev("ws_turned"), l + 1)
                    note(v.tensor_copy(wsT[:, l, :, :], bank[(7, 1)[l]][:, :].rearrange("p (h i) -> p h i", h=SH)))
                settle()
                v.memset(wsT[64:P, :, :, 0:64].rearrange("p l h i -> p (l h) i"), 0.0).then_inc(ev("const_vec"), 1)
                dve.wait_ge(ev("const_vec"), N_VEC)
                dve.wait_ge(ev("chan_out"), 3)

            ahead(stages[0])
            for st in stages:
                k = st["kind"]
                norm(st)
                if k == "post":
                    continue
                if st["M"] == 0:
                    constants()
                if k == "mix1":
                    mix1(st)
                elif k == "mix2":
                    mix2(st)
                elif k == "moe":
                    router(st)
                    experts(main, st, 0)
                    flag = dve.value_load(spill[0:1, 0:1])
                    with dve.If(flag > 0):
                        experts(again, SPILL, 1)
                        dve.nop()
                    dve.end_ifs()
                    ahead(after(st))
                    mark(x_done, TT)
                else:
                    ffn(st)
                    add_down(st, 1.0 if k == "ffn1" else 0.5, st["B"] + 3 * st["n"])


N_SMALL = 8
N_POOL = 4
N_VEC = 2

NAMES = [
    "x", "norm1_g", "w_in", "pool_w", "pool_scale", "sgu_ln_g", "sgu_ln_b", "sgu_w", "sgu_b", "conv_w", "group_g",
    "w_out", "norm2_g", "ffn_w_gate", "ffn_w_up", "ffn_w_down", "router_w", "router_b", "moe_w_gate", "moe_w_up",
    "moe_w_down", "final_g", "ffn1_norm_2", "ffn1_w_gate_2", "ffn1_w_up_2", "ffn1_w_down_2", "mix_norm_2",
    "w_in_2", "q_latent_norm_2", "w_uq_2", "kv_latent_norm_2", "w_ukv_2", "q_norm_2", "k_norm_2", "conv_w_2",
    "conv_b_2", "conv_ln_g_2", "conv_ln_b_2", "w_out_2", "ffn2_norm_2", "ffn2_w_gate_2", "ffn2_w_up_2",
    "ffn2_w_down_2", "post_norm_2",
]


def kernel(**inputs):
    import concourse.bacc as bacc
    from concourse.bass_utils import run_bass_kernel_spmd as run

    nc = bacc.Bacc("TRN2", target_bir_lowering=False, num_devices=1)
    arrays, A = {}, {}
    for name in NAMES:
        a = np.ascontiguousarray(inputs[name])
        arrays[f"in_{name}"] = a
        A[name] = nc.dram_tensor(f"in_{name}", a.shape, mybir.dt.from_np(a.dtype), kind="ExternalInput").ap()
    arrays["rope_table"] = rope_tables()
    rope = nc.dram_tensor("rope_table", (T, ROPE), F32, kind="ExternalInput").ap()
    out = nc.dram_tensor("out", (1, T, D), F32, kind="ExternalOutput").ap()
    build(nc, A, rope, out)
    return run(nc, [arrays], core_ids=[0]).results[0]["out"]
```
